# Optimizing a Trainium2 kernel written in Bass

```python
import jax, jax.numpy as jnp
from jax import lax
import numpy as np

D_MODEL = 1024
BATCH = 1
SEQ = 512
DEPTH = 2

N_A = DEPTH // 2
N_B = DEPTH - N_A
M_HEADS = 4
M_QK = D_MODEL // (2 * M_HEADS)
M_V = D_MODEL // M_HEADS
M_CHUNK = 64
GATE_CAP = 15.0
M_IN = 2 * M_HEADS * M_QK + 2 * D_MODEL + 2 * M_HEADS
F_HEADS = 16
F_HD = D_MODEL // F_HEADS
Q_BLOCK = 128
KV_OUT = 2 * D_MODEL + F_HEADS
D_FF = ((-(-8 * D_MODEL // 3) + 255) // 256) * 256
EPS = 1e-6

kernel_name = "yoco_mlstm_fox_hybrid"

def rmsnorm(x, g):
    xf = x.astype(jnp.float32)
    y = xf * lax.rsqrt(jnp.mean(xf * xf, axis=-1, keepdims=True) + EPS)
    return (y * g.astype(jnp.float32)).astype(x.dtype)

def softcap(a, cap):
    return cap * jnp.tanh(a / cap)

def mlstm_chunkwise(q, k, v, ig, lf):
    B, H, S, dk = q.shape
    dv = v.shape[-1]
    L = M_CHUNK
    nc = S // L
    q = q * dk ** -0.5

    def to_chunks(a):
        return jnp.moveaxis(a.reshape(B, H, nc, L, *a.shape[3:]), 2, 0)

    qc, kc, vc, ic, fc = (to_chunks(a) for a in (q, k, v, ig, lf))
    causal = jnp.tril(jnp.ones((L, L), dtype=bool))

    def step(carry, inp):
        C, n, m = carry
        qb, kb, vb, ib, fb = inp
        b = jnp.cumsum(fb, axis=-1)
        dmat = jnp.where(causal, b[..., :, None] - b[..., None, :] + ib[..., None, :], -jnp.inf)
        inter = b + m[..., None]
        m_t = jnp.maximum(inter, jnp.max(dmat, axis=-1))
        w = jnp.exp(dmat - m_t[..., None])
        a = jnp.exp(inter - m_t)
        s = jnp.einsum('bhtd,bhsd->bhts', qb, kb) * w
        num = a[..., None] * jnp.einsum('bhtd,bhde->bhte', qb, C) + jnp.einsum('bhts,bhse->bhte', s, vb)
        den = a * jnp.einsum('bhtd,bhd->bht', qb, n) + jnp.sum(s, axis=-1)
        h = num / jnp.maximum(jnp.abs(den), jnp.exp(-m_t))[..., None]
        bl = b[..., -1]
        ws = bl[..., None] - b + ib
        m_new = jnp.maximum(bl + m, jnp.max(ws, axis=-1))
        a_c = jnp.exp(bl + m - m_new)
        ws = jnp.exp(ws - m_new[..., None])
        C = a_c[..., None, None] * C + jnp.einsum('bhs,bhsd,bhse->bhde', ws, kb, vb)
        n = a_c[..., None] * n + jnp.einsum('bhs,bhsd->bhd', ws, kb)
        return (C, n, m_new), h

    init = (jnp.zeros((B, H, dk, dv), jnp.float32), jnp.zeros((B, H, dk), jnp.float32),
            jnp.zeros((B, H), jnp.float32))
    _, h = lax.scan(step, init, (qc, kc, vc, ic, fc))
    return jnp.moveaxis(h, 0, 2).reshape(B, H, S, dv)

def mlstm_mixer(h, w_in, gate_b, hn_g, w_out):
    B, S, _ = h.shape
    dq = M_HEADS * M_QK
    proj = h @ w_in
    q, k, v, o, gi, gf = jnp.split(
        proj, [dq, 2 * dq, 2 * dq + D_MODEL, 2 * dq + 2 * D_MODEL, 2 * dq + 2 * D_MODEL + M_HEADS], axis=-1)
    heads = lambda a, d: a.reshape(B, S, M_HEADS, d).transpose(0, 2, 1, 3).astype(jnp.float32)
    q, k, v = heads(q, M_QK), heads(k, M_QK), heads(v, M_V)
    ig = softcap((gi + gate_b[:M_HEADS]).astype(jnp.float32), GATE_CAP).transpose(0, 2, 1)
    lf = jax.nn.log_sigmoid(softcap((gf + gate_b[M_HEADS:]).astype(jnp.float32), GATE_CAP)).transpose(0, 2, 1)
    hh = mlstm_chunkwise(q, k, v, ig, lf)
    hh = hh * lax.rsqrt(jnp.mean(hh * hh, axis=-1, keepdims=True) + EPS)
    hh = hh.transpose(0, 2, 1, 3).reshape(B, S, D_MODEL) * hn_g.astype(jnp.float32)
    y = jax.nn.sigmoid(o.astype(jnp.float32)) * hh
    return y.astype(h.dtype) @ w_out

def shared_kv(x, cs, g, mod_w, mod_b, w, f_b):
    B, S, _ = x.shape
    sh, sc = jnp.split((cs @ mod_w + mod_b)[:, None, :], 2, axis=-1)
    h = rmsnorm(x, g) * (1 + sc) + sh
    p = h @ w
    k, v, fg = jnp.split(p, [D_MODEL, 2 * D_MODEL], axis=-1)
    heads = lambda a: a.reshape(B, S, F_HEADS, F_HD).transpose(0, 2, 1, 3)
    logf = jax.nn.log_sigmoid((fg + f_b).astype(jnp.float32))
    F = jnp.cumsum(logf, axis=1).transpose(0, 2, 1)
    return heads(k), heads(v), F

def fox_attention(q, k, v, F):
    S = q.shape[2]
    scale = F_HD ** -0.5
    outs = []
    for i in range(S // Q_BLOCK):
        q0, q1 = i * Q_BLOCK, (i + 1) * Q_BLOCK
        qb, kb, vb = q[:, :, q0:q1], k[:, :, :q1], v[:, :, :q1]
        logits = (jnp.einsum('bhqd,bhkd->bhqk', qb, kb).astype(jnp.float32) * scale
                  + F[:, :, q0:q1, None] - F[:, :, None, :q1])
        mask = (q0 + jnp.arange(Q_BLOCK))[:, None] >= jnp.arange(q1)[None, :]
        p = jax.nn.softmax(jnp.where(mask, logits, -jnp.inf), axis=-1).astype(vb.dtype)
        outs.append(jnp.einsum('bhqk,bhkd->bhqd', p, vb))
    return jnp.concatenate(outs, axis=2)

def fox_mixer(h, k, v, F, w_q, w_out):
    B, S, _ = h.shape
    q = (h @ w_q).reshape(B, S, F_HEADS, F_HD).transpose(0, 2, 1, 3)
    o = fox_attention(q, k, v, F)
    return o.transpose(0, 2, 1, 3).reshape(B, S, D_MODEL) @ w_out

def swiglu(h, w_in, w_out):
    g, u = jnp.split(h @ w_in, 2, axis=-1)
    return (jax.nn.silu(g) * u) @ w_out

def setup_inputs(seed: int = 0) -> dict:
    key = jax.random.key(seed)
    ks = iter(jax.random.split(key, 32))
    D = D_MODEL
    nrm = lambda shape, s: jax.random.normal(next(ks), shape, jnp.float32) * s
    return {
        "x": nrm((BATCH, SEQ, D), 1.0),
        "c": nrm((BATCH, D), 1.0),
        "mod_w": nrm((DEPTH, D, 6 * D), D ** -0.5),
        "mod_b": nrm((DEPTH, 6 * D), 0.02),
        "mix_pre_g": 1.0 + nrm((DEPTH, D), 0.02),
        "mix_post_g": 1.0 + nrm((DEPTH, D), 0.02),
        "ffn_pre_g": 1.0 + nrm((DEPTH, D), 0.02),
        "ffn_post_g": 1.0 + nrm((DEPTH, D), 0.02),
        "ffn_w_in": nrm((DEPTH, D, 2 * D_FF), D ** -0.5),
        "ffn_w_out": nrm((DEPTH, D_FF, D), D_FF ** -0.5),
        "a_w_in": nrm((N_A, D, M_IN), D ** -0.5),
        "a_gate_b": nrm((N_A, 2 * M_HEADS), 0.02),
        "a_hnorm_g": 1.0 + nrm((N_A, D), 0.02),
        "a_w_out": nrm((N_A, D, D), D ** -0.5),
        "kv_norm_g": 1.0 + nrm((D,), 0.02),
        "kv_mod_w": nrm((D, 2 * D), D ** -0.5),
        "kv_mod_b": nrm((2 * D,), 0.02),
        "kv_w": nrm((D, KV_OUT), D ** -0.5),
        "kv_fgate_b": nrm((F_HEADS,), 0.02),
        "b_w_q": nrm((N_B, D, D), D ** -0.5),
        "b_w_out": nrm((N_B, D, D), D ** -0.5),
    }

def reference(x, c, mod_w, mod_b, mix_pre_g, mix_post_g, ffn_pre_g, ffn_post_g, ffn_w_in, ffn_w_out,
              a_w_in, a_gate_b, a_hnorm_g, a_w_out, kv_norm_g, kv_mod_w, kv_mod_b, kv_w, kv_fgate_b,
              b_w_q, b_w_out):
    cs = jax.nn.silu(c)
    k_sh = v_sh = F_sh = None
    for l in range(DEPTH):
        sh1, sc1, g1, sh2, sc2, g2 = jnp.split((cs @ mod_w[l] + mod_b[l])[:, None, :], 6, axis=-1)
        h = rmsnorm(x, mix_pre_g[l]) * (1 + sc1) + sh1
        if l < N_A:
            y = mlstm_mixer(h, a_w_in[l], a_gate_b[l], a_hnorm_g[l], a_w_out[l])
        else:
            if l == N_A:
                k_sh, v_sh, F_sh = shared_kv(x, cs, kv_norm_g, kv_mod_w, kv_mod_b, kv_w, kv_fgate_b)
            y = fox_mixer(h, k_sh, v_sh, F_sh, b_w_q[l - N_A], b_w_out[l - N_A])
        x = x + g1 * rmsnorm(y, mix_post_g[l])
        h = rmsnorm(x, ffn_pre_g[l]) * (1 + sc2) + sh2
        x = x + g2 * rmsnorm(swiglu(h, ffn_w_in[l], ffn_w_out[l]), ffn_post_g[l])
    return x


_drawn_inputs = setup_inputs


def setup_inputs(seed=0):
    import zlib

    import numpy as np

    out = dict(_drawn_inputs(seed))
    spreads = {}
    factors = {'mix_post_g': 3.698,
     'ffn_pre_g': 3.455,
     'ffn_post_g': 4.344,
     'a_gate_b': 8.0,
     'a_hnorm_g': 4.951,
     'kv_norm_g': 6.351,
     'kv_mod_b': 5.334,
     'kv_fgate_b': 22.258}
    for name, (base, spread) in spreads.items():
        noise = np.random.default_rng([zlib.crc32(name.encode()), seed]).standard_normal(out[name].shape)
        drawn = base * np.exp(spread * noise) if base else spread * noise
        out[name] = __import__('jax').numpy.asarray(drawn.astype(out[name].dtype))
    for name, factor in factors.items():
        out[name] = (out[name] * factor).astype(out[name].dtype)
    return out
```

```python
from contextlib import ExitStack

import numpy as np

import concourse.bass as bass
from concourse import mybir

F32 = mybir.dt.float32
F32R = mybir.dt.float32r
BF16 = mybir.dt.bfloat16
ALU = mybir.AluOpType
ACT = mybir.ActivationFunctionType
AX_X = mybir.AxisListType.X
ds = bass.ds

P = 128
D = 1024
S = 512
KT = D // P
TT = S // P
HALF = 512
MH = 4
DK = D // (2 * MH)
DV = D // MH
FH = 16
HD = D // FH
PAIRS = FH // 2
FF = 2816
FT = FF // P
CAP = 15.0
EPS = 1e-6
WBIG = 2 * D
WSMALL = D
MIXBLK = 16
BIG = MIXBLK + FT
PERL = BIG + FT
UNITS = 14
NEG = -1.0e30
FREE = 1
(SH1_0, SC1_0, G1_0, SH2_0, SC2_0, G2_0, KVSH, KVSC, SH1_1, SC1_1, G1_1, SH2_1, SC2_1, G2_1) = range(UNITS)
ACC = 5
GAINS = ["mix0", "ffn0", "kv", "mix1", "ffn1", "hn", "c"]
CB = UNITS * KT
COL = {n: CB + i * KT for i, n in enumerate(GAINS)}
CMG = CB + len(GAINS) * KT
CFG = CMG + 1
NCOL = CFG + 1


class Chain:

    def __init__(self, eng, sem):
        self.eng, self.sem, self.base, self.k, self.i, self.per = eng, sem, 0, 0, None, 0

    def loop(self, i, per):
        self.base, self.i, self.per, self.k = self.base + self.k, i, per, 0

    def end(self, trips):
        assert self.k == self.per, (self.k, self.per)
        self.base, self.i, self.k, self.per = self.base + trips * self.per, None, 0, 0

    def __call__(self, ins):
        self.k += 1
        ins.then_inc(self.sem, 1)
        return ins

    def wait(self):
        n = self.base + self.k
        self.eng.wait_ge(self.sem, n if self.i is None else self.i * self.per + n)


def build(nc, x_in, wbig, wsmall, mods, cols, rows, gw0, gw1, out):
    ctx = ExitStack()
    with ctx:
        def sb(name, shape, dt=F32):
            return ctx.enter_context(nc.sbuf_tensor(name, shape, dt))

        sems = {}

        def sem(name):
            if name not in sems:
                sems[name] = ctx.enter_context(nc.semaphore(name))
            return sems[name]

        x = sb("x", [P, TT, D])
        h_hi = sb("h_hi", [P, KT, S], F32R)
        h_lo = sb("h_lo", [P, KT, S], F32R)
        w_raw = sb("w_raw", [P, 2, WBIG])
        w_hi = sb("w_hi", [P, 2, WBIG], F32R)
        w_lo = sb("w_lo", [P, 2, WBIG], F32R)
        m_raw = sb("m_raw", [P, 2, D])
        acc = sb("acc", [P, ACC, D])
        brow = sb("brow", [P, 2, D])
        xn = sb("xn", [P, D])
        junk = sb("junk", [P, D], BF16)
        ct = sb("ct", [P, NCOL])
        cs = sb("cs", [P, KT])
        gsc = sb("gsc", [P, KT])
        gsh = sb("gsh", [P, KT])
        gs2 = sb("gs2", [P, 4, 2, KT])
        st = sb("st", [P, 8, TT])
        ident = sb("ident", [P, P])
        ones = sb("ones", [P, P])
        identb = sb("identb", [P, P], BF16)
        trib = sb("trib", [P, 2, P], BF16)
        epsc = sb("epsc", [P, 1])
        gwr = sb("gwr", [P, KT, 36])
        gwh = sb("gwh", [P, KT, 36], F32R)
        gwl = sb("gwl", [P, KT, 36], F32R)
        hb = sb("hb", [P, 2, HALF])

        a0 = (nc.sbuf_base + 31) // 32 * 32
        room = nc.sbuf_usable_end - a0

        def place(tag, want):
            at, got = a0, {}
            for name, shape, dt in want:
                size = int(np.prod(shape[1:])) * (2 if dt == BF16 else 4)
                got[name] = nc.alloc_sbuf_tensor_at(f"{tag}_{name}", shape, dt, offset=at)
                at += (size + 31) // 32 * 32
            assert at - a0 <= room, (tag, at - a0, room)
            return got

        A = place("a", [("qk", [P, 8, S], F32), ("v", [P, TT, MH, DV + 1], F32), ("og", [P, TT, D], F32),
                        ("sT", [P, TT, S], F32), ("Mp", [P, S], F32), ("gc", [P, TT, 36], F32)])
        A["wT"] = acc[:, 0, :].rearrange("p (a n) -> p a n", a=2)
        A["kst"], A["Mh"] = acc[:, 1, 0:S], acc[:, 1, S:2 * S]
        off = a0 + (8 * S + TT * MH * (DV + 1) + TT * D) * 4
        G = {}
        for i, name in enumerate(["th", "L", "nB", "G2"]):
            G[name] = nc.alloc_sbuf_tensor_at(f"g_{name}", [P, S], F32, offset=off + i * S * 4)
        B = place("b", [("k", [P, PAIRS, S], F32), ("v", [P, TT, D], F32), ("q", [P, PAIRS, S], F32),
                        ("PT", [P, TT, S], F32), ("nF", [P, S], F32)])
        B["Pm"] = m_raw[:, 0, :].rearrange("p (a n) -> p a n", a=2)
        B["qst"] = m_raw[:, 1, :].rearrange("p (a n) -> p a n", a=2)
        B["nFm"] = acc[:, 4, :].rearrange("p (a n) -> p a n", a=2)
        B["vst"] = xn[:, 0:TT * P].rearrange("p (a n) -> p a n", a=TT)
        offb = a0 + (PAIRS * S + TT * D + PAIRS * S) * 4
        GB = {}
        for i, name in enumerate(["a", "mn", "L"]):
            GB[name] = nc.alloc_sbuf_tensor_at(f"gb_{name}", [P, S], F32, offset=offb + i * S * 4)
        F = place("f", [("act", [P, FT, S], F32), ("sg", [P, 2, S], F32), ("ahi", [P, 2, S], F32R),
                        ("alo", [P, 2, S], F32R)])

        ps = ctx.enter_context(nc.psum_tensor("ps", [P, 8, HALF], F32))

        w_in = [sem("w_in0"), sem("w_in1")]
        whi_ok = [sem("whi_ok0"), sem("whi_ok1")]
        wlo_ok = [sem("wlo_ok0"), sem("wlo_ok1")]
        w_used = [sem("w_used0"), sem("w_used1")]
        m_in = [sem("m_in0"), sem("m_in1")]
        m_used = [sem("m_used0"), sem("m_used1")]
        acc_ok = sem("acc_ok")
        consts_in, rows_in, x_in_ok = sem("consts_in"), sem("rows_in"), sem("x_in_ok")
        setup_pool, setup_dve = sem("setup_pool"), sem("setup_dve")

        block = ctx.enter_context(nc.Block())

        @block.sync
        def _(sp):
            sp.dma_start(ct[:], cols).then_inc(consts_in, 16)
            for one in whi_ok + wlo_ok + w_used:
                sp.sem_inc(one, FREE)
            for name in ("act0_0", "act0_1", "act1_0", "act1_1", "kq", "sT_0", "sT_1", "E", "num", "wT", "yh",
                         "S_mm", "ov", "PTps0", "PTps1", "Pe", "PT", "o"):
                sp.sem_inc(sem(name), FREE)
            for tt in range(TT):
                sp.dma_start(x[:, tt, :], x_in[tt * P:(tt + 1) * P, :]).then_inc(x_in_ok, 16)
            sp.dma_start(gwr[:], gw0).then_inc(sem("gw_in"), 16)

            def load(src, width, index, slot, order):
                sp.wait_ge(whi_ok[slot], order + FREE)
                sp.wait_ge(wlo_ok[slot], order + FREE)
                sp.dma_start(w_raw[:, slot, 0:width],
                             src[ds(index, 1)].rearrange("a p n -> p (a n)")).then_inc(w_in[slot], 16)

            for l in range(2):
                if l == 1:
                    sp.wait_ge(sem("gw_split"), 1)
                    sp.dma_start(gwr[:], gw1).then_inc(sem("gw_in"), 16)
                with sp.Fori(0, BIG // 2) as i:
                    for s in range(2):
                        load(wbig, WBIG, l * BIG + 2 * i + s, s, l * PERL // 2 + i)
                with sp.Fori(0, FT // 2) as i:
                    for s in range(2):
                        load(wsmall, WSMALL, l * FT + 2 * i + s, s, (l * PERL + BIG) // 2 + i)
            for tt in range(TT):
                sp.wait_ge(sem("x_new3"), tt + 1)
                sp.dma_start(out[tt * P:(tt + 1) * P, :], x[:, tt, :]).then_inc(sem("stored"), 16)
            sp.wait_ge(sem("stored"), 16 * TT)

        @block.gpsimd
        def _(pool):
            g = nc.gpsimd
            chain = Chain(pool, sem("pool_self"))
            chain(g.memset(ident[:], 0.0))
            chain(g.memset(identb[:], 0.0))
            chain(g.memset(trib[:], 0.0))
            chain(g.memset(ones[:], 1.0))
            chain(g.memset(epsc[:], EPS))
            chain.wait()
            for m in (ident, identb):
                chain(g.affine_select(out=m[:], in_=m[:], compare_op=ALU.not_equal, fill=1.0, base=0,
                                      pattern=[[-1, P]], channel_multiplier=1))
            chain(g.affine_select(out=trib[:, 0, :], in_=trib[:, 0, :], compare_op=ALU.is_ge, fill=NEG, base=0,
                                  pattern=[[1, P]], channel_multiplier=-1))
            chain(g.affine_select(out=trib[:, 1, :], in_=trib[:, 1, :], compare_op=ALU.is_ge, fill=NEG, base=0,
                                  pattern=[[-1, P]], channel_multiplier=1))
            chain.wait()
            g.engine_nop().then_inc(setup_pool, 1)

            def split(slot, width, order):
                pool.wait_ge(whi_ok[slot], order + 1 + FREE)
                pool.wait_ge(w_used[slot], order + FREE)
                g.tensor_tensor(w_lo[:, slot, 0:width], w_raw[:, slot, 0:width],
                                w_hi[:, slot, 0:width].bitcast(F32), ALU.subtract).then_inc(wlo_ok[slot], 1)

            for l in range(2):
                with pool.Fori(0, BIG // 2) as i:
                    for s in range(2):
                        split(s, WBIG, l * PERL // 2 + i)
                with pool.Fori(0, FT // 2) as i:
                    for s in range(2):
                        split(s, WSMALL, (l * PERL + BIG) // 2 + i)

        @block.scalar
        def _(act):
            a = nc.scalar
            me = Chain(act, sem("act_self"))

            def cast(slot, width, order):
                act.wait_ge(w_in[slot], 16 * (order + 1))
                act.wait_ge(w_used[slot], order + FREE)
                a.copy(w_hi[:, slot, 0:width], w_raw[:, slot, 0:width]).then_inc(whi_ok[slot], 1)

            def fetch(index, slot, order):
                act.wait_ge(m_used[slot], order)
                act.dma_start(m_raw[:, slot, :], mods[ds(index, 1)].rearrange("a p n -> p (a n)")
                              ).then_inc(m_in[slot], 16)

            def fetch_unit(u, last=False):
                for j in range(KT - 2 * last):
                    fetch(u * KT + j + 2, j % 2, u * (KT // 2) + j // 2 + 1)

            def fetch_rows(n, before):
                if before:
                    act.wait_ge(sem("gp_ok"), before)
                act.dma_start(brow[:], rows[n].partition_broadcast(P)).then_inc(rows_in, 16)

            def square_sum(src, col, tt, n, sem_std):
                me(a.activation(junk[:, 0:D], src, ACT.Square, accum_out=st[:, col, tt:tt + 1]))
                me.wait()
                a.activation(st[:, col + 1, tt:tt + 1], st[:, col, tt:tt + 1], ACT.Sqrt, bias=epsc[:],
                             scale=1.0 / n).then_inc(sem_std, 1)

            def affine(tag, tt, scale, shift):
                for f2 in range(2):
                    n = 2 * tt + f2
                    act.wait_ge(sem(f"tr{tag}"), n + 1)
                    if n >= 2:
                        act.wait_ge(sem(f"h{tag}"), n - 1)
                    for f in range(4):
                        k = 4 * f2 + f
                        a.activation(hb[:, f2, f * P:(f + 1) * P], ps[:, 2 * tt + f2, f * P:(f + 1) * P],
                                     ACT.Identity, scale=scale[:, k:k + 1],
                                     bias=(shift[:, k:k + 1] if shift is not None else 0.0)
                                     ).then_inc(sem(f"hb{tag}"), 1)

            def resid_norm(r, tag, scale, shift):
                order = [("y", 0), ("y", 1), ("x", 0), ("y", 2), ("x", 1), ("y", 3), ("x", 2), ("x", 3)]
                done = []
                for kind, tt in order:
                    if kind == "y":
                        act.wait_ge(sem(f"y{r}"), tt + 1)
                        square_sum(ps[:, 2 * tt:2 * tt + 2, :], 0, tt, D, sem(f"ystd{r}"))
                    elif tag is not None:
                        act.wait_ge(sem(f"x_new{r}"), tt + 1)
                        square_sum(x[:, tt, :], 3, tt, D, sem(f"xstd{tag}"))
                        done.append(tt)
                        if tt >= 1:
                            affine(tag, tt - 1, scale, shift)
                if tag is not None:
                    affine(tag, TT - 1, scale, shift)

            def ffn(l):
                base = l * PERL // 2 + MIXBLK // 2
                down = (l * PERL + BIG) // 2

                def body(n, width):
                    for s in range(2):
                        act.wait_ge(sem(f"g{l}"), 2 * n + s + 1)
                        act.wait_ge(sem(f"act{l}_{s}"), n + FREE)
                        a.activation(F["sg"][:, s, :], ps[:, 2 * s, :], ACT.Silu).then_inc(sem(f"sg{l}"), 1)
                        cast(s, width, base + n + 1)

                if l == 0:
                    with act.Fori(0, 5) as i:
                        body(2 * i, WBIG)
                        for j in range(KT):
                            fetch((G2_0 + i) * KT + j + 2, j % 2, (G2_0 + i) * (KT // 2) + j // 2 + 1)
                        body(2 * i + 1, WBIG)
                    body(10, WSMALL)
                else:
                    with act.Fori(0, FT // 2 - 1) as i:
                        body(i, WBIG)
                    body(FT // 2 - 1, WSMALL)
                with act.Fori(0, FT // 2 - 1) as i:
                    for s in range(2):
                        cast(s, WSMALL, down + i + 1)
                if l == 0:
                    for s in range(2):
                        cast(s, WBIG, PERL // 2)

            def keep(i, hh, tb):
                act.wait_ge(sem(f"PTps{tb % 2}"), 4 * i + 2 * hh + tb // 2 + 1 + FREE)
                if tb == 0:
                    act.wait_ge(sem("ov"), 2 * i + hh + FREE)
                a.copy(B["PT"][:, 0:tb + 1, tb * P:(tb + 1) * P],
                       ps[:, 2 + tb % 2, 0:(tb + 1) * P].rearrange("p (s t) -> p s t", s=tb + 1)
                       ).then_inc(sem("PT"), 1)

            act.wait_ge(consts_in, 16)
            a.activation(cs[:], ct[:, COL["c"]:COL["c"] + KT], ACT.Silu).then_inc(sem("cs"), 1)
            fetch(0, 0, 0)
            fetch(1, 1, 0)
            fetch_rows(0, 0)
            fetch_unit(SH1_0)
            fetch_unit(SC1_0)
            act.wait_ge(setup_pool, 1)
            act.wait_ge(x_in_ok, 16 * TT)
            for tt in range(TT):
                square_sum(x[:, tt, :], 3, tt, D, sem("xstd0"))
            for s in range(2):
                cast(s, WBIG, 0)
            act.wait_ge(sem("fin0"), 1)
            for tt in range(TT):
                affine("0", tt, gsc, gsh)

            for i in range(2):
                fetch_unit(G1_0 + i)
                for s in range(2):
                    cast(s, WBIG, i + 1)
            fetch_unit(SC2_0)
            act.wait_ge(sem("gate_mm0"), 1)
            act.wait_ge(sem("gb15"), 1)
            me(a.activation(G["th"][0:36, :], ps[0:36, 4, :], ACT.Tanh, scale=1.0 / CAP, bias=st[0:36, 6, 0:1]))
            me.wait()
            me(a.activation(G["L"][0:4, :], G["th"][32:36, :], ACT.Exp, scale=-CAP))
            me.wait()
            a.activation(G["L"][0:4, :], G["L"][0:4, :], ACT.Ln, bias=ones[0:4, 0:1]).then_inc(sem("lf"), 1)
            act.wait_ge(sem("nbm"), 1)
            a.activation(G["G2"][32:36, :], A["Mh"][0:4, :], ACT.Exp).then_inc(sem("em"), 1)
            for gg in range(4):
                for s in range(2):
                    cast(s, WBIG, 3 + gg)
                if gg >= 2:
                    act.wait_ge(w_used[1], 3 + gg + FREE)
                    for tt in range(TT):
                        a.activation(A["og"][:, tt, (gg - 2) * HALF:(gg - 1) * HALF], ps[:, 4 * (gg % 2) + tt, :],
                                     ACT.Sigmoid).then_inc(sem("og"), 1)
            with act.Fori(0, MH) as h:
                act.wait_ge(sem("kq"), 4 * h + FREE)
                a.copy(A["kst"], A["qk"][:, ds(MH + h, 1), :].rearrange("p a n -> p (a n)")
                       ).then_inc(sem("kst"), 1)
                act.wait_ge(sem("E"), h + 1 + FREE)
                for sb_ in range(TT):
                    act.wait_ge(sem(f"sT_{sb_ % 2}"), 2 * h + sb_ // 2 + FREE)
                    last = a.activation(A["wT"][:, sb_ % 2, 0:P], ps[:, 3, sb_ * P:(sb_ + 1) * P], ACT.Exp,
                                        bias=A["gc"][:, sb_, ds(h, 1)])
                    if sb_ < TT - 1:
                        last = a.activation(A["wT"][:, sb_ % 2, P:S - sb_ * P], ps[:, 0, (sb_ + 1) * P:S], ACT.Exp,
                                            bias=A["gc"][:, sb_, ds(h, 1)])
                        last.then_inc(sem("wT"), 1)
                    else:
                        last.then_inc(sem("wT"), 1)
                act.wait_ge(sem("rden"), h + 1)
                for tt in range(TT):
                    a.activation(junk[:, tt * DV:(tt + 1) * DV], ps[:, 4 + tt, 0:DV], ACT.Square, scale=st[:, 2, tt:tt + 1],
                                 accum_out=st[:, 3, tt:tt + 1]).then_inc(sem("hsq"), 1)
                act.wait_ge(sem("hsq"), TT * (h + 1))
                a.activation(st[:, 4, :], st[:, 3, :], ACT.Sqrt, bias=epsc[:], scale=1.0 / DV
                             ).then_inc(sem("hstd"), 1)
            for tt in range(TT):
                affine("y0", tt, ct[:, COL["hn"]:COL["hn"] + KT], None)
            for i in range(2):
                for s in range(2):
                    cast(s, WBIG, 7 + i)
            fetch_rows(1, 1)
            resid_norm(0, "1", gs2[:, 0, 0, :], gs2[:, 0, 1, :])
            ffn(0)
            fetch_rows(2, 2)
            resid_norm(1, "2", gs2[:, 1, 0, :], gs2[:, 1, 1, :])

            b0 = PERL // 2
            for i in range(2):
                fetch_unit(G1_1 + i)
                for s in range(2):
                    cast(s, WBIG, b0 + 1 + i)
            act.wait_ge(sem("gate_mm1"), 1)
            fb = ct[0:FH, CFG:CFG + 1]
            me(a.activation(GB["a"][0:FH, :], ps[0:FH, 4, :], ACT.Abs, bias=fb))
            me.wait()
            me(a.activation(GB["L"][0:FH, :], GB["a"][0:FH, :], ACT.Exp, scale=-1.0))
            me.wait()
            a.activation(GB["L"][0:FH, :], GB["L"][0:FH, :], ACT.Ln, bias=ones[0:FH, 0:1]).then_inc(sem("lf1"), 1)
            for gg in range(2):
                for s in range(2):
                    cast(s, WBIG, b0 + 3 + gg)
            for tt in range(TT):
                affine("q", tt, gs2[:, 2, 0, :], gs2[:, 2, 1, :])
            for i in range(2):
                fetch_unit(SC2_1 + i, last=(i == 1))
                for s in range(2):
                    cast(s, WBIG, b0 + 5 + i)
            act.wait_ge(sem("qst0"), 1)
            act.wait_ge(sem("q"), 4)
            with act.Fori(0, PAIRS) as i:
                act.wait_ge(sem("S_mm"), 8 * i + FREE)
                act.wait_ge(sem("ov"), 2 * i + FREE)
                for hh in range(2):
                    r = slice(64 * hh, 64 * hh + 64)
                    a.copy(B["qst"][r, hh, :], B["q"][r, ds(i, 1), :].rearrange("p a n -> p (a n)")
                           ).then_inc(sem("qst"), 1)
                a.copy(B["vst"], B["v"][:, :, ds(i * P, P)]).then_inc(sem("vst"), 1)
                for hh in range(2):
                    for tb in range(TT):
                        n = 4 * hh + tb
                        act.wait_ge(sem("nmax"), 8 * i + n + 1)
                        act.wait_ge(sem(f"PTps{tb % 2}"), 4 * i + n // 2 + FREE)
                        a.activation(B["Pm"][:, tb % 2, 0:(tb + 1) * P], ps[:, tb % 2, 0:(tb + 1) * P], ACT.Exp,
                                     bias=st[:, 0, tb:tb + 1], accum_out=st[:, 1, tb:tb + 1]
                                     ).then_inc(sem("Pe"), 1)
                        if tb >= 1:
                            keep(i, hh, tb - 1)
                    keep(i, hh, TT - 1)
            for i in range(2):
                for s in range(2):
                    cast(s, WBIG, b0 + 7 + i)
            fetch_rows(3, 3)
            resid_norm(2, "3", gs2[:, 0, 0, :], gs2[:, 0, 1, :])
            ffn(1)
            resid_norm(3, None, None, None)

        @block.vector
        def _(dve):
            v = nc.vector
            me = Chain(dve, sem("dve_self"))
            mult, add, sub, mx = ALU.mult, ALU.add, ALU.subtract, ALU.max

            def unit(u, a_slot):
                for j in range(KT):
                    dve.wait_ge(m_in[j % 2], 16 * (u * (KT // 2) + j // 2 + 1))
                    c = cs[:, j:j + 1]
                    dst = (acc[:, a_slot, :] if isinstance(a_slot, int)
                           else acc[:, ds(a_slot, 1), :].rearrange("p a n -> p (a n)"))
                    if j == 0:
                        ins = v.tensor_scalar(dst, m_raw[:, 0, :], c, None, mult)
                    else:
                        dve.wait_ge(m_used[(j - 1) % 2], u * (KT // 2) + (j - 1) // 2 + 1)
                        ins = v.scalar_tensor_tensor(dst, m_raw[:, j % 2, :], c, dst, mult, add)
                    ins.then_inc(m_used[j % 2], 1)

            def fin_cols(psb, u_sh, u_sc, gain, dst_g, dst_s):
                me(v.tensor_tensor(dst_s, psb[:, 0:KT], ct[:, u_sh * KT:(u_sh + 1) * KT], add))
                me(v.tensor_tensor(st[:, 6:8, :].rearrange("p a n -> p (a n)"), psb[:, KT:2 * KT],
                                   ct[:, u_sc * KT:(u_sc + 1) * KT], add))
                me.wait()
                return v.scalar_tensor_tensor(dst_g, st[:, 6:8, :].rearrange("p a n -> p (a n)"), 1.0,
                                              ct[:, COL[gain]:COL[gain] + KT], add, mult)

            def fin_gate(banks, a_slot, n):
                dve.wait_ge(rows_in, 16 * (n + 1))
                me(v.tensor_tensor(acc[:, a_slot, :], ps[:, banks:banks + 2, :].rearrange("p a n -> p (a n)"),
                                   brow[:, 0, :], add))
                me.wait()
                return v.tensor_tensor(acc[:, a_slot, :], acc[:, a_slot, :], brow[:, 1, :], mult)

            def normalise(tag, tt):
                dve.wait_ge(sem(f"xstd{tag}"), tt + 1)
                me(v.reciprocal(st[:, 5, tt:tt + 1], st[:, 4, tt:tt + 1]))
                me.wait()
                emit_xn(tag, tt)

            def emit_xn(tag, tt):
                if tt >= 1:
                    dve.wait_ge(sem(f"tr{tag}"), 2 * tt)
                v.tensor_scalar(xn[:], x[:, tt, :], st[:, 5, tt:tt + 1], None, mult).then_inc(sem(f"xn{tag}"), 1)

            def split(tag, tt):
                for f2 in range(2):
                    dve.wait_ge(sem(f"hb{tag}"), 4 * (2 * tt + f2 + 1))
                    src = hb[:, f2, :].rearrange("p (f t) -> p f t", f=4)
                    hi = h_hi[:, 4 * f2:4 * f2 + 4, tt * P:(tt + 1) * P]
                    lo = h_lo[:, 4 * f2:4 * f2 + 4, tt * P:(tt + 1) * P]
                    me(v.tensor_copy(hi, src))
                    me.wait()
                    v.tensor_tensor(lo, src, hi.bitcast(F32), sub).then_inc(sem(f"h{tag}"), 1)

            def update(r, tt, gp):
                dve.wait_ge(sem(f"ystd{r}"), tt + 1)
                me(v.reciprocal(st[:, 2, tt:tt + 1], st[:, 1, tt:tt + 1]))
                me.wait()
                v.scalar_tensor_tensor(xn[:], ps[:, 2 * tt:2 * tt + 2, :].rearrange("p a n -> p (a n)"),
                                       st[:, 2, tt:tt + 1], acc[:, gp, :], mult, mult
                                       ).then_inc(sem(f"yread{r}"), 1)
                dve.wait_ge(sem(f"yread{r}"), tt + 1)
                v.tensor_tensor(x[:, tt, :], x[:, tt, :], xn[:], add).then_inc(sem(f"x_new{r}"), 1)

            def resid_norm(r, tag, gp):
                if tag is None:
                    for tt in range(TT):
                        update(r, tt, gp)
                        dve.wait_ge(sem(f"x_new{r}"), tt + 1)
                    return
                for tt in range(TT):
                    if tt >= 1:
                        dve.wait_ge(sem(f"tr{tag}"), 2 * tt)
                    update(r, tt, gp)
                    normalise_after(r, tag, tt)
                    if tt >= 1:
                        split(tag, tt - 1)
                split(tag, TT - 1)

            def normalise_after(r, tag, tt):
                dve.wait_ge(sem(f"x_new{r}"), tt + 1)
                normalise(tag, tt)

            def ffn(l):
                def tile(n, s):
                    dve.wait_ge(w_used[s], l * PERL // 2 + MIXBLK // 2 + n + 1 + FREE)
                    dve.wait_ge(sem(f"sg{l}"), 2 * n + s + 1)
                    v.tensor_tensor(F["act"][:, ds(2 * n + s, 1), :].rearrange("p a n -> p (a n)"),
                                    F["sg"][:, s, :], ps[:, 2 * s + 1, :], mult).then_inc(sem(f"act{l}_{s}"), 1)

                if l == 0:
                    with dve.Fori(0, 5) as i:
                        for s in range(2):
                            tile(2 * i, s)
                        unit(G2_0 + i, i)
                        for s in range(2):
                            tile(2 * i + 1, s)
                    for s in range(2):
                        tile(10, s)
                else:
                    with dve.Fori(0, FT // 2) as i:
                        for s in range(2):
                            tile(i, s)
                dve.wait_ge(sem(f"gp_mm{2 * l + 1}"), 1)
                fin_gate(4, (G2_0, G2_1)[l] % ACC, 2 * l + 1).then_inc(sem("gp_ok"), 1)
                if l == 0:
                    fin_cols(ps[:, 6, 0:16], KVSH, KVSC, "kv", gs2[:, 1, 0, :], gs2[:, 1, 1, :]
                             ).then_inc(sem("fin2a"), 1)
                    dve.wait_ge(sem("fin2a"), 1)
                    fin_cols(ps[:, 6, 16:32], SH1_1, SC1_1, "mix1", gs2[:, 2, 0, :], gs2[:, 2, 1, :]
                             ).then_inc(sem("fin2"), 1)
                with dve.Fori(0, FT // 2) as i:
                    for s in range(2):
                        dve.wait_ge(sem(f"act{l}_{s}"), FT // 2 + FREE)
                        dve.wait_ge(w_used[s], (l * PERL + BIG) // 2 + i + FREE)
                        src = F["act"][:, ds(2 * i + s, 1), :].rearrange("p a n -> p (a n)")
                        v.tensor_copy(F["ahi"][:, s, :], src).then_inc(sem(f"ahi{l}_{s}"), 1)
                        dve.wait_ge(sem(f"ahi{l}_{s}"), i + 1)
                        v.tensor_tensor(F["alo"][:, s, :], src, F["ahi"][:, s, :].bitcast(F32), sub
                                        ).then_inc(sem(f"alo{l}_{s}"), 1)

            dve.wait_ge(consts_in, 16)
            dve.wait_ge(sem("cs"), 1)
            unit(SH1_0, SH1_0)
            unit(SC1_0, SC1_0)
            dve.wait_ge(m_used[1], KT)
            v.engine_nop().then_inc(acc_ok, 1)
            dve.wait_ge(sem("fin_mm0"), 1)
            fin_cols(ps[:, 0, 0:16], SH1_0, SC1_0, "mix0", gsc[:], gsh[:]).then_inc(sem("fin0a"), 1)
            dve.wait_ge(sem("fin0a"), 1)
            me(v.tensor_scalar(st[0:36, 6, 0:1], ct[0:36, CMG:CMG + 1], 1.0 / CAP, None, mult)
               )
            me.wait()
            v.engine_nop().then_inc(sem("fin0"), 1)
            v.engine_nop().then_inc(sem("gb15"), 1)
            for tt in range(TT):
                normalise("0", tt)
                if tt >= 1:
                    split("0", tt - 1)
            split("0", TT - 1)
            dve.wait_ge(sem("gw_in"), 16)
            me(v.tensor_copy(gwh[:], gwr[:]))
            me.wait()
            v.tensor_tensor(gwl[:], gwr[:], gwh[:].bitcast(F32), sub).then_inc(sem("gw_split"), 1)

            for i in range(2):
                unit(G1_0 + i, (G1_0 + i) % ACC)
                for s in range(2):
                    n = 2 * i + s
                    dve.wait_ge(w_used[s], i + 1 + FREE)
                    v.tensor_copy(A["qk"][:, 2 * n:2 * n + 2, :], ps[:, 2 * s:2 * s + 2, :]).then_inc(sem("qk"), 1)
            unit(SC2_0, SC2_0 % ACC)
            me(v.memset(A["Mp"][:], 0.0))
            me(v.memset(A["v"][:, :, :, DV:DV + 1], 1.0))
            me(v.memset(G["G2"][0:64, :], 0.0))
            dve.wait_ge(sem("lf"), 1)
            me.wait()
            me(v.memset(A["Mh"], 1.0))
            me.wait()
            me(v.tensor_tensor_scan(G["nB"][0:4, :], A["Mh"][0:4, :], G["L"][0:4, :], 0.0, mult, add))
            me.wait()
            me(v.scalar_tensor_tensor(G["G2"][0:4, :], G["th"][0:4, :], CAP, G["nB"][0:4, :], mult, add))
            me.wait()
            me(v.tensor_tensor_scan(A["Mp"][0:4, :], A["Mh"][0:4, :], G["G2"][0:4, :], 0.0, mult, mx))
            me.wait()
            v.tensor_tensor(A["Mh"][0:4, :], G["nB"][0:4, :], A["Mp"][0:4, :], sub).then_inc(sem("nbm"), 1)
            dve.wait_ge(sem("nbm"), 1)
            for gg in range(2):
                dve.wait_ge(w_used[1], 3 + gg + FREE)
                for tt in range(TT):
                    v.tensor_copy(A["v"][:, tt, 2 * gg:2 * gg + 2, 0:DV],
                                  ps[:, 4 * (gg % 2) + tt, :].rearrange("p (h n) -> p h n", h=2)
                                  ).then_inc(sem("v"), 1)
            dve.wait_ge(sem("gt_mm"), 1)
            me(v.tensor_copy(A["gc"][:], ps[:, 3, 0:TT * 36].rearrange("p (t n) -> p t n", t=TT)))
            me.wait()
            v.engine_nop().then_inc(sem("gc"), 1)
            with dve.Fori(0, MH) as h:
                me.loop(h, 3)
                dve.wait_ge(sem("E"), h + FREE)
                v.tensor_scalar(A["Mh"], A["Mp"][:], ident[:, ds(h, 1)], -1.0, mult, mult
                                ).then_inc(sem("Mh"), 1)
                for sb_ in range(TT):
                    n = S - sb_ * P
                    dve.wait_ge(sem("kq"), 4 * h + sb_ + 1 + FREE)
                    dve.wait_ge(sem("wT"), 4 * h + sb_ + 1 + FREE)
                    dve.wait_ge(sem("num"), h + FREE)
                    v.scalar_tensor_tensor(A["sT"][:, sb_, sb_ * P:S], ps[:, 1 + sb_ % 2, 0:n], float(DK) ** -0.5,
                                           A["wT"][:, sb_ % 2, 0:n], mult, mult).then_inc(sem(f"sT_{sb_ % 2}"), 1)
                dve.wait_ge(sem("num"), h + 1 + FREE)
                den = ps[:, 4:8, DV:DV + 1].rearrange("p t o -> p (t o)")
                em = A["gc"][:, :, ds(32 + h, 1)].rearrange("p t o -> p (t o)")
                me(v.scalar_tensor_tensor(st[:, 0, :], den, -1.0, em, mult, mx))
                me.wait()
                me(v.tensor_tensor(st[:, 1, :], den, st[:, 0, :], mx))
                me.wait()
                v.reciprocal(st[:, 2, :], st[:, 1, :]).then_inc(sem("rden"), 1)
                dve.wait_ge(sem("hstd"), h + 1)
                dve.wait_ge(sem("rden"), h + 1)
                me(v.reciprocal(st[:, 5, :], st[:, 4, :]))
                me.wait()
                v.tensor_tensor(st[:, 5, :], st[:, 5, :], st[:, 2, :], mult).then_inc(sem("hscale"), 1)
                dve.wait_ge(sem("hscale"), h + 1)
                dve.wait_ge(sem("og"), 8)
                for tt in range(TT):
                    o = A["og"][:, tt, ds(h * DV, DV)]
                    v.scalar_tensor_tensor(o, ps[:, 4 + tt, 0:DV], st[:, 5, tt:tt + 1], o, mult, mult
                                           ).then_inc(sem("yh"), 1)
            me.end(MH)
            for tt in range(TT):
                split("y0", tt)
            dve.wait_ge(sem("gp_mm0"), 1)
            fin_gate(0, G1_0 % ACC, 0).then_inc(sem("gp_ok"), 1)
            fin_cols(ps[:, 2, 0:16], SH2_0, SC2_0, "ffn0", gs2[:, 0, 0, :], gs2[:, 0, 1, :]
                     ).then_inc(sem("fin1"), 1)
            resid_norm(0, "1", G1_0 % ACC)
            ffn(0)
            resid_norm(1, "2", G2_0 % ACC)

            dve.wait_ge(sem("gw_in"), 32)
            me(v.tensor_copy(gwh[:], gwr[:]))
            me.wait()
            v.tensor_tensor(gwl[:], gwr[:], gwh[:].bitcast(F32), sub).then_inc(sem("gw_split"), 1)
            for i in range(2):
                unit(G1_1 + i, i)
                for s in range(2):
                    n = 2 * i + s
                    dve.wait_ge(w_used[s], PERL // 2 + i + 1 + FREE)
                    v.tensor_copy(B["k"][:, 2 * n:2 * n + 2, :], ps[:, 2 * s:2 * s + 2, :]).then_inc(sem("k"), 1)
            me(v.memset(B["nF"][:], 0.0))
            dve.wait_ge(sem("lf1"), 1)
            me(v.tensor_scalar(GB["mn"][0:FH, :], ps[0:FH, 4, :], ct[0:FH, CFG:CFG + 1], 0.0, add, ALU.min))
            me.wait()
            me(v.tensor_tensor(GB["L"][0:FH, :], GB["L"][0:FH, :], GB["mn"][0:FH, :], sub))
            me(v.memset(GB["a"][0:FH, :], 1.0))
            me.wait()
            v.tensor_tensor_scan(B["nF"][0:FH, :], GB["a"][0:FH, :], GB["L"][0:FH, :], 0.0, mult, add
                                 ).then_inc(sem("nF"), 1)
            for gg in range(2):
                dve.wait_ge(w_used[1], PERL // 2 + 3 + gg + FREE)
                for tt in range(TT):
                    v.tensor_copy(B["v"][:, tt, gg * HALF:(gg + 1) * HALF], ps[:, 4 * (gg % 2) + tt, :]
                                  ).then_inc(sem("v1"), 1)
            for tt in range(TT):
                emit_xn("q", tt)
                if tt >= 1:
                    split("q", tt - 1)
            split("q", TT - 1)
            for i in range(2):
                unit(SC2_1 + i, 2 + i)
                for s in range(2):
                    n = 2 * i + s
                    dve.wait_ge(w_used[s], PERL // 2 + 4 + i + 1 + FREE)
                    v.tensor_scalar(B["q"][:, 2 * n:2 * n + 2, :], ps[:, 2 * s:2 * s + 2, :], float(HD) ** -0.5,
                                    None, mult).then_inc(sem("q"), 1)
            dve.wait_ge(m_used[1], UNITS * KT // 2)
            v.memset(B["qst"], 0.0).then_inc(sem("qst0"), 1)
            dve.wait_ge(sem("nF"), 1)
            with dve.Fori(0, PAIRS) as i:
                me.loop(i, 11)
                for hh in range(2):
                    dve.wait_ge(sem("S_mm"), 8 * i + FREE)
                    v.tensor_scalar(B["nFm"][:, hh, :], B["nF"][:], ident[:, ds(2 * i + hh, 1)], None, mult
                                    ).then_inc(sem("nFm"), 1)
                for hh in range(2):
                    for tb in range(TT):
                        n = (tb + 1) * P
                        m = 4 * hh + tb
                        dve.wait_ge(sem("S_mm"), 8 * i + m + 1 + FREE)
                        v.tensor_reduce(st[:, 0, tb:tb + 1], ps[:, tb % 2, 0:n], AX_X, mx, negate=True
                                        ).then_inc(sem("nmax"), 1)
                        dve.wait_ge(sem("Pe"), 8 * i + m + 1 + FREE)
                        me(v.reciprocal(st[:, 2, tb:tb + 1], st[:, 1, tb:tb + 1]))
                        me.wait()
                        v.tensor_scalar(B["Pm"][:, tb % 2, 0:n], B["Pm"][:, tb % 2, 0:n], st[:, 2, tb:tb + 1],
                                        None, mult).then_inc(sem("Pn"), 1)
                    dve.wait_ge(sem("ov"), 2 * i + hh + 1 + FREE)
                    dve.wait_ge(sem("o"), i + FREE)
                    r = slice(64 * hh, 64 * hh + 64)
                    me(v.tensor_copy(hb[r, 0, :], ps[r, 4 + hh, :]))
                me.wait()
                hi = h_hi[:, ds(i, 1), :].rearrange("p a n -> p (a n)")
                me(v.tensor_copy(hi, hb[:, 0, :]))
                me.wait()
                v.tensor_tensor(h_lo[:, ds(i, 1), :].rearrange("p a n -> p (a n)"), hb[:, 0, :],
                                hi.bitcast(F32), sub).then_inc(sem("o"), 1)
            me.end(PAIRS)
            dve.wait_ge(sem("gp_mm2"), 1)
            fin_gate(0, G1_1 % ACC, 2).then_inc(sem("gp_ok"), 1)
            fin_cols(ps[:, 2, 0:16], SH2_1, SC2_1, "ffn1", gs2[:, 0, 0, :], gs2[:, 0, 1, :]
                     ).then_inc(sem("fin3"), 1)
            resid_norm(2, "3", G1_1 % ACC)
            ffn(1)
            resid_norm(3, None, G2_1 % ACC)

        @block.tensor
        def _(pe):
            t = nc.tensor

            def parts(order, s):
                pe.wait_ge(whi_ok[s], order + 1 + FREE)
                pe.wait_ge(wlo_ok[s], order + 1 + FREE)

            def three(dst, l_hi, l_lo, r_hi, r_lo, start, stop):
                t.matmul(dst, l_hi, r_lo, start=start, stop=False)
                t.matmul(dst, l_lo, r_hi, start=False, stop=False)
                return t.matmul(dst, l_hi, r_hi, start=False, stop=stop)

            def features(order, s, bank):
                parts(order, s)
                whi = w_hi[:, s, :].rearrange("p (k n) -> p k n", k=KT)
                wlo = w_lo[:, s, :].rearrange("p (k n) -> p k n", k=KT)
                for m in range(2):
                    for k in range(KT):
                        last = three(ps[:, bank + m, :], whi[:, k, m * P:(m + 1) * P], wlo[:, k, m * P:(m + 1) * P],
                                     h_hi[:, k, :], h_lo[:, k, :], k == 0, k == KT - 1)
                last.then_inc(w_used[s], 1)

            def tokens(order, bank):
                for s in range(2):
                    parts(order, s)
                    whi = w_hi[:, s, :].rearrange("p (k n) -> p k n", k=4)
                    wlo = w_lo[:, s, :].rearrange("p (k n) -> p k n", k=4)
                    for tt in range(TT):
                        for k4 in range(4):
                            k = 4 * s + k4
                            c = slice(tt * P, (tt + 1) * P)
                            last = three(ps[:, bank + tt, :], h_hi[:, k, c], h_lo[:, k, c], whi[:, k4, :],
                                         wlo[:, k4, :], k == 0, k == KT - 1)
                    last.then_inc(w_used[s], 1)

            def adaln_cols(bank, col, unit):
                for f in range(KT):
                    last = t.matmul(ps[:, bank, col + f:col + f + 1], acc[:, unit % ACC, f * P:(f + 1) * P],
                                    ones[:, 0:1], start=True, stop=True)
                return last

            def adaln_row(bank, unit):
                for half in range(2):
                    last = t.matmul(ps[:, bank + half, :], ones[:], acc[:, unit % ACC, half * HALF:(half + 1) * HALF],
                                    start=True, stop=True)
                return last

            def transpose(tag, src_ok, src, free):
                for tt in range(TT):
                    if src_ok is not None:
                        pe.wait_ge(src_ok[0], src_ok[1] * (tt + 1))
                    if free is not None:
                        free(tt)
                    for f2 in range(2):
                        for f in range(4):
                            k = 4 * f2 + f
                            last = t.transpose(ps[:, 2 * tt + f2, f * P:(f + 1) * P], src(tt, k), ident[:])
                        last.then_inc(sem(f"tr{tag}"), 1)

            def xn_tile(tt, k):
                return xn[:, k * P:(k + 1) * P]

            def gate_mm(m, done):
                for k in range(KT):
                    last = three(ps[0:m, 4, :], gwh[:, k, 0:m], gwl[:, k, 0:m], h_hi[:, k, :], h_lo[:, k, :],
                                 k == 0, k == KT - 1)
                last.then_inc(done, 1)

            def out_proj(order, r):
                for g in range(2):
                    for s in range(2):
                        parts(order + g, s)
                        whi = w_hi[:, s, :].rearrange("p (k n) -> p k n", k=4)
                        wlo = w_lo[:, s, :].rearrange("p (k n) -> p k n", k=4)
                        for tt in range(TT):
                            for k4 in range(4):
                                k = 4 * s + k4
                                c = slice(tt * P, (tt + 1) * P)
                                last = three(ps[:, 2 * tt + g, :], h_hi[:, k, c], h_lo[:, k, c], whi[:, k4, :],
                                             wlo[:, k4, :], k == 0, k == KT - 1)
                            if g == 1 and s == 1:
                                last.then_inc(sem(f"y{r}"), 1)
                        if g == 0 or s == 0:
                            last.then_inc(w_used[s], 1)
                last_used(1, f"y{r}")

            def last_used(s, y):
                pe.wait_ge(sem(y), TT)
                pe.sem_inc(w_used[s], 1)

            def ffn(l):
                base = l * PERL // 2 + MIXBLK // 2
                down = (l * PERL + BIG) // 2
                r = 2 * l + 1
                pe.wait_ge(sem(f"h{r}"), 2 * TT)
                with pe.Fori(0, FT // 2) as i:
                    for s in range(2):
                        parts(base + i, s)
                        pe.wait_ge(sem(f"act{l}_{s}"), i + FREE)
                        whi = w_hi[:, s, :].rearrange("p (k n) -> p k n", k=KT)
                        wlo = w_lo[:, s, :].rearrange("p (k n) -> p k n", k=KT)
                        for m in range(2):
                            for k in range(KT):
                                last = three(ps[:, 2 * s + m, :], whi[:, k, m * P:(m + 1) * P],
                                             wlo[:, k, m * P:(m + 1) * P], h_hi[:, k, :], h_lo[:, k, :],
                                             k == 0, k == KT - 1)
                            if m == 0:
                                last.then_inc(sem(f"g{l}"), 1)
                        last.then_inc(w_used[s], 1)
                last = adaln_row(4, (G2_0, G2_1)[l])
                if l == 0:
                    for n, u in enumerate((KVSH, KVSC, SH1_1, SC1_1)):
                        last = adaln_cols(6, KT * n, u)
                last.then_inc(sem(f"gp_mm{r}"), 1)
                for s in range(2):
                    pe.wait_ge(sem(f"act{l}_{s}"), FT // 2 + FREE)
                pe.wait_ge(sem("gp_ok"), 2 * l + 2)
                if l == 0:
                    pe.wait_ge(sem("fin2"), 1)

                def ktile(i, s, start, stop):
                    parts(down + i, s)
                    pe.wait_ge(sem(f"alo{l}_{s}"), i + 1)
                    for tt in range(TT):
                        c = slice(tt * P, (tt + 1) * P)
                        for half in range(2):
                            n = slice(half * HALF, (half + 1) * HALF)
                            last = three(ps[:, 2 * tt + half, :], F["ahi"][:, s, c], F["alo"][:, s, c],
                                         w_hi[:, s, n], w_lo[:, s, n], start, stop)
                        if stop:
                            last.then_inc(sem(f"y{r}"), 1)
                    if not stop:
                        last.then_inc(w_used[s], 1)

                ktile(0, 0, True, False)
                ktile(0, 1, False, False)
                with pe.Fori(1, FT // 2 - 1) as i:
                    for s in range(2):
                        ktile(i, s, False, False)
                ktile(FT // 2 - 1, 0, False, False)
                ktile(FT // 2 - 1, 1, False, True)
                last_used(1, f"y{r}")

            pe.wait_ge(acc_ok, 1)
            pe.wait_ge(setup_pool, 1)
            adaln_cols(0, 0, SH1_0)
            adaln_cols(0, KT, SC1_0).then_inc(sem("fin_mm0"), 1)
            pe.wait_ge(sem("fin0"), 1)
            transpose("0", (sem("xn0"), 1), xn_tile, None)
            pe.wait_ge(sem("h0"), 2 * TT)
            for i in range(2):
                for s in range(2):
                    n = 2 * i + s
                    if i:
                        pe.wait_ge(sem("qk"), n - 1)
                    features(i, s, 2 * s)
            pe.wait_ge(sem("gw_split"), 1)
            gate_mm(36, sem("gate_mm0"))
            pe.wait_ge(sem("qk"), 4)
            tokens(2, 0)
            pe.wait_ge(sem("lf"), 1)
            tokens(3, 4)
            pe.wait_ge(sem("v"), 4)
            tokens(4, 0)
            pe.wait_ge(sem("v"), 8)
            tokens(5, 4)
            pe.wait_ge(sem("og"), 4)
            pe.wait_ge(sem("em"), 1)
            for tt in range(TT):
                last = t.transpose(ps[:, 3, tt * 36:(tt + 1) * 36], G["G2"][0:36, tt * P:(tt + 1) * P],
                                   ident[0:36, 0:36])
            last.then_inc(sem("gt_mm"), 1)
            pe.wait_ge(sem("og"), 8)
            pe.wait_ge(sem("gc"), 1)
            with pe.Fori(0, MH) as h:
                pe.wait_ge(sem("wT"), 4 * h + FREE)
                pe.wait_ge(sem("Mh"), h + 1)
                t.matmul(ps[:, 0, :], ones[:], A["Mh"], start=True, stop=True)
                t.matmul(ps[:, 3, :], ones[:], A["Mh"], start=True, stop=False)
                for tb in range(TT):
                    last = t.matmul(ps[:, 3, tb * P:(tb + 1) * P], identb[:], trib[:, 0, :], start=False,
                                    stop=tb == TT - 1)
                last.then_inc(sem("E"), 1)
                pe.wait_ge(sem("kst"), h + 1)
                for sb_ in range(TT):
                    q = A["qk"][:, ds(h, 1), :].rearrange("p a n -> p (a n)")[:, sb_ * P:S]
                    if sb_ >= 2:
                        pe.wait_ge(sem(f"sT_{sb_ % 2}"), 2 * h + sb_ // 2 + FREE)
                    else:
                        pe.wait_ge(sem(f"sT_{sb_ % 2}"), 2 * h + FREE)
                    t.matmul(ps[:, 1 + sb_ % 2, 0:S - sb_ * P], A["kst"][:, sb_ * P:(sb_ + 1) * P], q,
                             start=True, stop=True).then_inc(sem("kq"), 1)
                for p_ in range(2):
                    pe.wait_ge(sem(f"sT_{p_}"), 2 * h + 2 + FREE)
                pe.wait_ge(sem("yh"), 4 * h + FREE)
                for tt in range(TT):
                    for sb_ in range(tt + 1):
                        last = t.matmul(ps[:, 4 + tt, 0:DV + 1], A["sT"][:, sb_, tt * P:(tt + 1) * P],
                                        A["v"][:, sb_, ds(h, 1), :].rearrange("p a n -> p (a n)"),
                                        start=sb_ == 0, stop=sb_ == tt)
                last.then_inc(sem("num"), 1)
            pe.wait_ge(sem("yh"), 16 + FREE)
            transpose("y0", None, lambda tt, k: A["og"][:, tt, k * P:(k + 1) * P], None)
            pe.wait_ge(sem("hy0"), 2 * TT)
            adaln_row(0, G1_0)
            adaln_cols(2, 0, SH2_0)
            adaln_cols(2, KT, SC2_0).then_inc(sem("gp_mm0"), 1)
            pe.wait_ge(sem("fin1"), 1)
            pe.wait_ge(sem("gp_ok"), 1)
            out_proj(6, 0)
            transpose("1", (sem("xn1"), 1), xn_tile, None)
            ffn(0)
            transpose("2", (sem("xn2"), 1), xn_tile, None)

            b0 = PERL // 2
            pe.wait_ge(sem("h2"), 2 * TT)
            for i in range(2):
                for s in range(2):
                    if i:
                        pe.wait_ge(sem("k"), 2 * i + s - 1)
                    features(b0 + i, s, 2 * s)
            pe.wait_ge(sem("gw_split"), 2)
            gate_mm(FH, sem("gate_mm1"))
            pe.wait_ge(sem("k"), 4)
            tokens(b0 + 2, 0)
            pe.wait_ge(sem("nF"), 1)
            tokens(b0 + 3, 4)
            pe.wait_ge(sem("v1"), 8)
            transpose("q", (sem("xnq"), 1), xn_tile, None)
            pe.wait_ge(sem("hq"), 2 * TT)
            for i in range(2):
                for s in range(2):
                    if i:
                        pe.wait_ge(sem("q"), 2 * i + s - 1)
                    features(b0 + 4 + i, s, 2 * s)
            pe.wait_ge(sem("q"), 4)
            with pe.Fori(0, PAIRS) as i:
                kp = B["k"][:, ds(i, 1), :].rearrange("p a n -> p (a n)")

                def scores(hh, tb):
                    m = 4 * hh + tb
                    n = (tb + 1) * P
                    pe.wait_ge(sem("Pe"), 8 * i + max(m - 1, 0) + FREE)
                    t.matmul(ps[:, tb % 2, 0:n], B["qst"][:, hh, tb * P:n], kp[:, 0:n], start=True, stop=False)
                    t.matmul(ps[:, tb % 2, 0:n], ones[:], B["nFm"][:, hh, 0:n], start=False, stop=False)
                    t.matmul(ps[:, tb % 2, n - P:n], identb[:], trib[:, 1, :], start=False, stop=True
                             ).then_inc(sem("S_mm"), 1)

                def turn(hh, tb):
                    m = 4 * hh + tb
                    pe.wait_ge(sem("Pn"), 8 * i + m + 1)
                    pe.wait_ge(sem("PT"), 8 * i + max(m - 1, 0) + FREE)
                    for sb_ in range(tb + 1):
                        last = t.transpose(ps[:, 2 + tb % 2, sb_ * P:(sb_ + 1) * P],
                                           B["Pm"][:, tb % 2, sb_ * P:(sb_ + 1) * P], ident[:])
                    last.then_inc(sem(f"PTps{tb % 2}"), 1)

                pe.wait_ge(sem("qst"), 2 * i + 2)
                for hh in range(2):
                    pe.wait_ge(sem("nFm"), 2 * i + hh + 1)
                    scores(hh, 0)
                    scores(hh, 1)
                    turn(hh, 0)
                    scores(hh, 2)
                    turn(hh, 1)
                    scores(hh, 3)
                    turn(hh, 2)
                    turn(hh, 3)
                    pe.wait_ge(sem("vst"), i + 1)
                    pe.wait_ge(sem("PT"), 8 * i + 4 * hh + 4 + FREE)
                    pe.wait_ge(sem("o"), i + FREE)
                    for sb_ in range(TT):
                        last = t.matmul(ps[:, 4 + hh, sb_ * P:S], B["vst"][:, sb_, :], B["PT"][:, sb_, sb_ * P:S],
                                        start=sb_ == 0, stop=sb_ == TT - 1)
                    last.then_inc(sem("ov"), 1)
            pe.wait_ge(sem("o"), PAIRS + FREE)
            adaln_row(0, G1_1)
            adaln_cols(2, 0, SH2_1)
            adaln_cols(2, KT, SC2_1).then_inc(sem("gp_mm2"), 1)
            pe.wait_ge(sem("fin3"), 1)
            pe.wait_ge(sem("gp_ok"), 3)
            out_proj(b0 + 6, 2)
            transpose("3", (sem("xn3"), 1), xn_tile, None)
            ffn(1)


_SHAPE = (1, S, D)


def lay_out(a):
    f = np.float32

    def feat(w):
        n = w.shape[1] // (2 * P)
        return w.reshape(KT, P, n, 2 * P).transpose(2, 1, 0, 3).reshape(n, P, WBIG)

    def tok(w):
        n = w.shape[1] // HALF
        return w.reshape(2, 4, P, n, HALF).transpose(3, 0, 2, 1, 4).reshape(2 * n, P, WBIG)

    def up(w):
        return w.reshape(KT, P, 2, FT, P).transpose(3, 1, 0, 2, 4).reshape(FT, P, WBIG)

    aw, kw = a["a_w_in"][0], a["kv_w"]
    big = np.concatenate([
        feat(aw[:, :D]), tok(aw[:, D:3 * D]), tok(a["a_w_out"][0]), up(a["ffn_w_in"][0]),
        feat(kw[:, :D]), tok(kw[:, D:2 * D]), feat(a["b_w_q"][0]), tok(a["b_w_out"][0]), up(a["ffn_w_in"][1])])
    small = a["ffn_w_out"].reshape(2 * FT, P, D)
    order = [(0, 0), (0, 1), (0, 2), (0, 3), (0, 4), (0, 5), "k0", "k1", (1, 0), (1, 1), (1, 2), (1, 3), (1, 4), (1, 5)]
    mats, bias = [], []
    for o in order:
        m, b = (a["kv_mod_w"], a["kv_mod_b"]) if isinstance(o, str) else (a["mod_w"][o[0]], a["mod_b"][o[0]])
        j = int(o[1])
        mats.append(m[:, j * D:(j + 1) * D].reshape(KT, P, D))
        bias.append(b[j * D:(j + 1) * D])
    mods = np.concatenate(mats)
    gains = [a["mix_pre_g"][0], a["ffn_pre_g"][0], a["kv_norm_g"], a["mix_pre_g"][1], a["ffn_pre_g"][1],
             a["a_hnorm_g"][0], a["c"][0]]
    cols = np.zeros((P, NCOL), f)
    for i, vec in enumerate(bias + gains):
        cols[:, i * KT:(i + 1) * KT] = vec.reshape(KT, P).T
    cols[0:4, CMG] = a["a_gate_b"][0][:4]
    cols[32:36, CMG] = a["a_gate_b"][0][4:]
    cols[0:FH, CFG] = a["kv_fgate_b"]
    rows = np.stack([np.stack([bias[G1_0], a["mix_post_g"][0]]), np.stack([bias[G2_0], a["ffn_post_g"][0]]),
                     np.stack([bias[G1_1], a["mix_post_g"][1]]), np.stack([bias[G2_1], a["ffn_post_g"][1]])])
    gw0 = np.zeros((P, KT, 36), f)
    gate = aw[:, 3 * D:].reshape(KT, P, 2 * MH).transpose(1, 0, 2)
    gw0[:, :, 0:4], gw0[:, :, 32:36] = gate[:, :, :4], gate[:, :, 4:]
    gw1 = np.zeros((P, KT, 36), f)
    gw1[:, :, 0:FH] = kw[:, 2 * D:].reshape(KT, P, FH).transpose(1, 0, 2)
    return {"x_in": a["x"][0], "wbig": big, "wsmall": small, "mods": mods, "cols": cols, "rows": rows,
            "gw0": gw0, "gw1": gw1}


def kernel(**inputs):
    import concourse.bacc as bacc
    from concourse.bass_utils import run_bass_kernel_spmd

    arrays = {n: np.ascontiguousarray(v) for n, v in
              lay_out({n: np.asarray(v) for n, v in inputs.items()}).items()}
    nc = bacc.Bacc("TRN2", target_bir_lowering=False, num_devices=1)
    aps = [nc.dram_tensor(f"in_{n}", v.shape, F32, kind="ExternalInput").ap() for n, v in arrays.items()]
    out = nc.dram_tensor("out_y", (S, D), F32, kind="ExternalOutput").ap()
    build(nc, *aps, out)
    r = run_bass_kernel_spmd(nc, [{f"in_{n}": v for n, v in arrays.items()}], core_ids=[0])
    return r.results[0]["out_y"].reshape(_SHAPE)
```

```python
from contextlib import ExitStack

import numpy as np

import concourse.bass as bass
from concourse import mybir

F32 = mybir.dt.float32
F32R = mybir.dt.float32r
BF16 = mybir.dt.bfloat16
ALU = mybir.AluOpType
ACT = mybir.ActivationFunctionType
AX_X = mybir.AxisListType.X
ds = bass.ds

P = 128
D = 1024
S = 512
KT = D // P
TT = S // P
HALF = 512
MH = 4
DK = D // (2 * MH)
DV = D // MH
FH = 16
HD = D // FH
PAIRS = FH // 2
FF = 2816
FT = FF // P
CAP = 15.0
EPS = 1e-6
WBIG = 2 * D
WSMALL = D
MIXBLK = 16
BIG = MIXBLK + FT
PERL = BIG + FT
UNITS = 14
NEG = -1.0e30
FREE = 1
(SH1_0, SC1_0, G1_0, SH2_0, SC2_0, G2_0, KVSH, KVSC, SH1_1, SC1_1, G1_1, SH2_1, SC2_1, G2_1) = range(UNITS)
ACC = 5
GAINS = ["mix0", "ffn0", "kv", "mix1", "ffn1", "hn", "c"]
CB = UNITS * KT
COL = {n: CB + i * KT for i, n in enumerate(GAINS)}
CMG = CB + len(GAINS) * KT
CFG = CMG + 1
NCOL = CFG + 1


class Chain:

    def __init__(self, eng, sem):
        self.eng, self.sem, self.base, self.k, self.i, self.per = eng, sem, 0, 0, None, 0

    def loop(self, i, per, start=0):
        self.base, self.i, self.per, self.k = self.base + self.k - start * per, i, per, 0
        self.start = start

    def end(self, trips):
        assert self.k == self.per, (self.k, self.per)
        self.base, self.i, self.k, self.per = self.base + (trips + self.start) * self.per, None, 0, 0

    def __call__(self, ins):
        self.k += 1
        ins.then_inc(self.sem, 1)
        return ins

    def wait(self):
        n = self.base + self.k
        self.eng.wait_ge(self.sem, n if self.i is None else self.i * self.per + n)


def build(nc, x_in, wbig, wsmall, mods, cols, rows, gw0, gw1, out):
    ctx = ExitStack()
    with ctx:
        def sb(name, shape, dt=F32):
            return ctx.enter_context(nc.sbuf_tensor(name, shape, dt))

        sems = {}

        def sem(name):
            if name not in sems:
                sems[name] = ctx.enter_context(nc.semaphore(name))
            return sems[name]

        x = sb("x", [P, TT, D])
        h_hi = sb("h_hi", [P, KT, S], F32R)
        h_lo = sb("h_lo", [P, KT, S], F32R)
        w_raw = sb("w_raw", [P, 2, WBIG])
        w_hi = sb("w_hi", [P, 2, WBIG], F32R)
        w_lo = sb("w_lo", [P, 2, WBIG], F32R)
        m_at = nc.sbuf_base
        m_raw = sb("m_raw", [P, 2, D])
        acc = sb("acc", [P, ACC, D])
        brow = sb("brow", [P, 2, D])
        xn = sb("xn", [P, D])
        junk = sb("junk", [P, D], BF16)
        ct = sb("ct", [P, NCOL])
        cs = sb("cs", [P, KT])
        gsc = sb("gsc", [P, KT])
        gsh = sb("gsh", [P, KT])
        gs2 = sb("gs2", [P, 4, 2, KT])
        st = sb("st", [P, 8, TT])
        ident = sb("ident", [P, P])
        ones = sb("ones", [P, P])
        ones_r = sb("ones_r", [P, P], F32R)
        two = sb("two", [P, FH + 4])
        hs = sb("hs", [P, 2, MH * TT])
        identb = sb("identb", [P, P], BF16)
        trib = sb("trib", [P, 2, P], BF16)
        epsc = sb("epsc", [P, 1])
        gwr = sb("gwr", [P, KT, 36])
        gwh = sb("gwh", [P, KT, 36], F32R)
        gwl = sb("gwl", [P, KT, 36], F32R)
        hb = sb("hb", [P, 2, HALF])
        xt = [xn[:], hb[:].rearrange("p a n -> p (a n)")]

        a0 = (nc.sbuf_base + 31) // 32 * 32
        room = nc.sbuf_usable_end - a0

        def place(tag, want):
            at, got = a0, {}
            for name, shape, dt in want:
                size = int(np.prod(shape[1:])) * (2 if dt == BF16 else 4)
                got[name] = nc.alloc_sbuf_tensor_at(f"{tag}_{name}", shape, dt, offset=at)
                at += (size + 31) // 32 * 32
            assert at - a0 <= room, (tag, at - a0, room)
            return got

        A = place("a", [("qk", [P, 8, S], F32), ("v", [P, TT, MH, DV + 1], F32), ("og", [P, TT, D], F32),
                        ("sT", [P, TT, S], F32), ("Mp", [P, S], F32R), ("gc", [P, TT, 36], F32)])
        acc_at = m_at + 2 * D * 4
        A["wT"] = acc[:, 0, :].rearrange("p (a n) -> p a n", a=2)
        A["kst"], A["w4"] = acc[:, 1, 0:S], acc[:, 1, S:2 * S]
        A["Mh"] = nc.alloc_sbuf_tensor_at("a_Mh", [P, S], F32R, offset=acc_at + (D + S) * 4)
        off = a0 + (8 * S + TT * MH * (DV + 1) + TT * D) * 4
        G = {}
        for i, name in enumerate(["th", "L", "nB", "G2"]):
            G[name] = nc.alloc_sbuf_tensor_at(f"g_{name}", [P, S], F32, offset=off + i * S * 4)
        B = place("b", [("k", [P, PAIRS, S], F32), ("v", [P, TT, D], F32), ("q", [P, PAIRS, S], F32),
                        ("PT", [P, TT, S], F32), ("nF", [P, S], F32R)])
        B["qhi"] = nc.alloc_sbuf_tensor_at("b_qhi", [P, 2, S], F32R, offset=m_at)
        B["qlo"] = nc.alloc_sbuf_tensor_at("b_qlo", [P, 2, S], F32R, offset=m_at + D * 4)
        B["nFm"] = nc.alloc_sbuf_tensor_at("b_nFm", [P, 2, S], F32R, offset=acc_at + 4 * D * 4)
        B["Pm"] = brow[:].rearrange("p a (b n) -> p (a b) n", b=2)
        B["vst"] = xn[:, 0:TT * P].rearrange("p (a n) -> p a n", a=TT)
        offb = a0 + (PAIRS * S + TT * D + PAIRS * S) * 4
        GB = {}
        for i, name in enumerate(["a", "mn", "L", "F"]):
            GB[name] = nc.alloc_sbuf_tensor_at(f"gb_{name}", [P, S], F32, offset=offb + i * S * 4)
        F = place("f", [("act", [P, FT, S], F32), ("sg", [P, 2, S], F32), ("ahi", [P, 2, S], F32R),
                        ("alo", [P, 2, S], F32R)])

        ps = ctx.enter_context(nc.psum_tensor("ps", [P, 8, HALF], F32))

        w_in = [sem("w_in0"), sem("w_in1")]
        whi_ok = [sem("whi_ok0"), sem("whi_ok1")]
        wlo_ok = [sem("wlo_ok0"), sem("wlo_ok1")]
        w_used = [sem("w_used0"), sem("w_used1")]
        m_in = [sem("m_in0"), sem("m_in1")]
        m_used = [sem("m_used0"), sem("m_used1")]
        acc_ok = sem("acc_ok")
        consts_in, rows_in, x_in_ok = sem("consts_in"), sem("rows_in"), sem("x_in_ok")
        setup_pool, setup_dve = sem("setup_pool"), sem("setup_dve")

        block = ctx.enter_context(nc.Block())

        @block.sync
        def _(sp):
            sp.dma_start(ct[:], cols).then_inc(consts_in, 16)
            for one in whi_ok + wlo_ok + w_used:
                sp.sem_inc(one, FREE)
            for name in ("act0_0", "act0_1", "act1_0", "act1_1", "yh"):
                sp.sem_inc(sem(name), FREE)
            for tt in range(TT):
                sp.dma_start(x[:, tt, :], x_in[tt * P:(tt + 1) * P, :]).then_inc(x_in_ok, 16)
            sp.dma_start(gwr[:], gw0).then_inc(sem("gw_in"), 16)

            def load(src, width, index, slot, order):
                sp.wait_ge(whi_ok[slot], order + FREE)
                sp.wait_ge(wlo_ok[slot], order + FREE)
                sp.dma_start(w_raw[:, slot, 0:width],
                             src[ds(index, 1)].rearrange("a p n -> p (a n)")).then_inc(w_in[slot], 16)

            for l in range(2):
                if l == 1:
                    sp.wait_ge(sem("gw_split"), 1)
                    sp.dma_start(gwr[:], gw1).then_inc(sem("gw_in"), 16)
                with sp.Fori(0, BIG // 2) as i:
                    for s in range(2):
                        load(wbig, WBIG, l * BIG + 2 * i + s, s, l * PERL // 2 + i)
                with sp.Fori(0, FT // 2) as i:
                    for s in range(2):
                        load(wsmall, WSMALL, l * FT + 2 * i + s, s, (l * PERL + BIG) // 2 + i)
            for tt in range(TT):
                sp.wait_ge(sem("x_new3"), tt + 1)
                sp.dma_start(out[tt * P:(tt + 1) * P, :], x[:, tt, :]).then_inc(sem("stored"), 16)
            sp.wait_ge(sem("stored"), 16 * TT)

        @block.gpsimd
        def _(pool):
            g = nc.gpsimd
            chain = Chain(pool, sem("pool_self"))
            chain(g.memset(ident[:], 0.0))
            chain(g.memset(identb[:], 0.0))
            chain(g.memset(trib[:], 0.0))
            chain(g.memset(ones[:], 1.0))
            chain(g.memset(epsc[:], EPS))
            chain.wait()
            for m in (ident, identb):
                chain(g.affine_select(out=m[:], in_=m[:], compare_op=ALU.not_equal, fill=1.0, base=0,
                                      pattern=[[-1, P]], channel_multiplier=1))
            chain(g.affine_select(out=trib[:, 0, :], in_=trib[:, 0, :], compare_op=ALU.is_ge, fill=NEG, base=0,
                                  pattern=[[1, P]], channel_multiplier=-1))
            chain(g.affine_select(out=trib[:, 1, :], in_=trib[:, 1, :], compare_op=ALU.is_ge, fill=NEG, base=0,
                                  pattern=[[-1, P]], channel_multiplier=1))
            chain.wait()
            g.engine_nop().then_inc(setup_pool, 1)

            def split(slot, width, order):
                pool.wait_ge(whi_ok[slot], order + 1 + FREE)
                pool.wait_ge(w_used[slot], order + FREE)
                g.tensor_tensor(w_lo[:, slot, 0:width], w_raw[:, slot, 0:width],
                                w_hi[:, slot, 0:width].bitcast(F32), ALU.subtract).then_inc(wlo_ok[slot], 1)

            for l in range(2):
                with pool.Fori(0, BIG // 2 if l == 0 else 7) as i:
                    for s in range(2):
                        split(s, WBIG, l * PERL // 2 + i)
                if l == 1:
                    def queries(i, hh, first):
                        r = slice(64 * hh, 64 * hh + 64)
                        pool.wait_ge(sem("qs"), i + 1)
                        if not first:
                            pool.wait_ge(sem("S_mm"), 8 * i - 4 + 4 * hh)
                            pool.wait_ge(sem("qlo"), 2 * i + hh)
                        g.tensor_tensor(B["qhi"][r, hh, :], hb[r, 0, :], hb[r, 1, :], ALU.add).then_inc(sem("qhi"), 1)
                        pool.wait_ge(sem("qhi"), 2 * i + hh + 1)
                        g.tensor_tensor(B["qlo"][r, hh, :], hb[r, 0, :], B["qhi"][r, hh, :].bitcast(F32),
                                        ALU.subtract).then_inc(sem("qlo"), 1)

                    pool.wait_ge(sem("k_hi"), 1)
                    pool.wait_ge(sem("qst0"), 1)
                    queries(0, 0, True)
                    for pairs in (slice(0, 1), slice(1, PAIRS)):
                        pool.wait_ge(sem("qlo"), 1)
                        g.tensor_tensor(h_lo[:, pairs, :], B["k"][:, pairs, :], h_hi[:, pairs, :].bitcast(F32),
                                        ALU.subtract).then_inc(sem("k_lo"), 1)
                    pool.wait_ge(sem("k_lo"), 2)
                    queries(0, 1, True)
                    with pool.Fori(1, PAIRS) as i:
                        for hh in range(2):
                            queries(i, hh, False)
                    pool.wait_ge(sem("qlo"), FH)
                    with pool.Fori(7, BIG // 2) as i:
                        for s in range(2):
                            split(s, WBIG, l * PERL // 2 + i)
                with pool.Fori(0, FT // 2) as i:
                    for s in range(2):
                        split(s, WSMALL, (l * PERL + BIG) // 2 + i)

        @block.scalar
        def _(act):
            a = nc.scalar
            me = Chain(act, sem("act_self"))

            def cast(slot, width, order):
                act.wait_ge(w_in[slot], 16 * (order + 1))
                act.wait_ge(w_used[slot], order + FREE)
                a.copy(w_hi[:, slot, 0:width], w_raw[:, slot, 0:width]).then_inc(whi_ok[slot], 1)

            def fetch(index, slot, order):
                act.wait_ge(m_used[slot], order)
                act.dma_start(m_raw[:, slot, :], mods[ds(index, 1)].rearrange("a p n -> p (a n)")
                              ).then_inc(m_in[slot], 16)

            def fetch_unit(u, chunks=range(KT)):
                for j in chunks:
                    if u * KT + j + 2 >= UNITS * KT:
                        break
                    fetch(u * KT + j + 2, j % 2, u * (KT // 2) + j // 2 + 1)

            def fetch_rows(n, before):
                if before:
                    act.wait_ge(sem("gp_ok"), before)
                act.dma_start(brow[:], rows[n].partition_broadcast(P)).then_inc(rows_in, 16)

            def square_sum(src, col, tt, n, sem_std):
                me(a.activation(junk[:, 0:D], src, ACT.Square, accum_out=st[:, col, tt:tt + 1]))
                me.wait()
                a.activation(st[:, col + 1, tt:tt + 1], st[:, col, tt:tt + 1], ACT.Sqrt, bias=epsc[:],
                             scale=1.0 / n).then_inc(sem_std, 1)

            def affine(tag, scale, shift):
                act.wait_ge(sem(f"tr{tag}"), TT)
                for f in range(KT):
                    if f >= 2:
                        act.wait_ge(sem(f"h{tag}"), f - 1)
                    a.activation(hb[:, f % 2, :], ps[:, f, :], ACT.Identity, scale=scale[:, f:f + 1],
                                 bias=(shift[:, f:f + 1] if shift is not None else 0.0)
                                 ).then_inc(sem(f"hb{tag}"), 1)

            def resid_norm(r, tag, scale, shift):
                order = [("y", 0), ("y", 1), ("x", 0), ("y", 2), ("x", 1), ("y", 3), ("x", 2), ("x", 3)]
                for kind, tt in order:
                    if kind == "y":
                        act.wait_ge(sem(f"y{r}"), tt + 1)
                        square_sum(ps[:, 2 * tt:2 * tt + 2, :], 0, tt, D, sem(f"ystd{r}"))
                    elif tag is not None:
                        act.wait_ge(sem(f"x_new{r}"), tt + 1)
                        square_sum(x[:, tt, :], 3, tt, D, sem(f"xstd{tag}"))
                if tag is not None:
                    affine(tag, scale, shift)

            def ffn(l):
                base = l * PERL // 2 + MIXBLK // 2
                down = (l * PERL + BIG) // 2

                def tile(n, s, width):
                    if True:
                        act.wait_ge(sem(f"g{l}"), 2 * n + s + 1)
                        act.wait_ge(sem(f"act{l}_{s}"), n + FREE)
                        a.activation(F["sg"][:, s, :], ps[:, 2 * s, :], ACT.Silu).then_inc(sem(f"sg{l}"), 1)
                        cast(s, width, base + n + 1)

                if l == 0:
                    with act.Fori(0, 5) as i:
                        for q in range(2):
                            for s in range(2):
                                tile(2 * i + q, s, WBIG)
                                for j in range(4 * q + 2 * s, 4 * q + 2 * s + 2):
                                    fetch((G2_0 + i) * KT + j + 2, j % 2, (G2_0 + i) * (KT // 2) + j // 2 + 1)
                    for s in range(2):
                        tile(10, s, WSMALL)
                else:
                    with act.Fori(0, FT // 2 - 1) as i:
                        for s in range(2):
                            tile(i, s, WBIG)
                    for s in range(2):
                        tile(FT // 2 - 1, s, WSMALL)
                with act.Fori(0, FT // 2 - 1) as i:
                    for s in range(2):
                        cast(s, WSMALL, down + i + 1)
                if l == 0:
                    for s in range(2):
                        cast(s, WBIG, PERL // 2)

            act.wait_ge(consts_in, 16)
            a.activation(cs[:], ct[:, COL["c"]:COL["c"] + KT], ACT.Silu).then_inc(sem("cs"), 1)
            fetch(0, 0, 0)
            fetch(1, 1, 0)
            fetch_rows(0, 0)
            fetch_unit(SH1_0)
            fetch_unit(SC1_0)
            act.wait_ge(setup_pool, 1)
            act.wait_ge(x_in_ok, 16 * TT)
            for tt in range(TT):
                square_sum(x[:, tt, :], 3, tt, D, sem("xstd0"))
            for s in range(2):
                cast(s, WBIG, 0)
            act.wait_ge(sem("fin0"), 1)
            affine("0", gsc, gsh)

            for i in range(2):
                for s in range(2):
                    fetch_unit(G1_0 + i, range(4 * s, 4 * s + 4))
                    cast(s, WBIG, i + 1)
            act.wait_ge(sem("gate_mm0"), 1)
            act.wait_ge(sem("gb15"), 1)
            me(a.activation(G["th"][0:36, :], ps[0:36, 4, :], ACT.Tanh, scale=1.0 / CAP, bias=st[0:36, 6, 0:1]))
            me.wait()
            me(a.activation(G["L"][0:4, :], G["th"][32:36, :], ACT.Exp, scale=-CAP))
            me.wait()
            a.activation(G["L"][0:4, :], G["L"][0:4, :], ACT.Ln, bias=ones[0:4, 0:1]).then_inc(sem("lf"), 1)
            act.wait_ge(sem("nbm"), 1)
            a.activation(G["G2"][32:36, :], A["w4"][0:4, :], ACT.Exp).then_inc(sem("em"), 1)
            for gg in range(4):
                if gg < 2:
                    fetch_unit(SC2_0, range(4 * gg, 4 * gg + 4))
                for s in range(2):
                    cast(s, WBIG, 3 + gg)
                if gg >= 2:
                    act.wait_ge(w_used[1], 3 + gg + FREE)
                    for tt in range(TT):
                        a.activation(A["og"][:, tt, (gg - 2) * HALF:(gg - 1) * HALF], ps[:, 4 * (gg % 2) + tt, :],
                                     ACT.Sigmoid).then_inc(sem("og"), 1)
            def keys(h):
                if not (isinstance(h, int) and h == 0):
                    act.wait_ge(sem("kq"), 4 * h)
                a.copy(A["kst"], A["qk"][:, ds(MH + h, 1), :].rearrange("p a n -> p (a n)")
                       ).then_inc(sem("kst"), 1)

            def decay(h, tiles):
                act.wait_ge(sem("E"), h + 1)
                for sb_ in tiles:
                    if not (isinstance(h, int) and h == 0 and sb_ < 2):
                        act.wait_ge(sem(f"sT_{sb_ % 2}"), 2 * h + sb_ // 2)
                    last = a.activation(A["wT"][:, sb_ % 2, 0:P], ps[:, 3, sb_ * P:(sb_ + 1) * P], ACT.Exp,
                                        bias=A["gc"][:, sb_, ds(h, 1)])
                    if sb_ < TT - 1:
                        last = a.activation(A["wT"][:, sb_ % 2, P:S - sb_ * P], ps[:, 0, (sb_ + 1) * P:S], ACT.Exp,
                                            bias=A["gc"][:, sb_, ds(h, 1)])
                    last.then_inc(sem("wT"), 1)

            def squares(h):
                act.wait_ge(sem("rden"), h + 1)
                for tt in range(TT):
                    a.activation(junk[:, tt * DV:(tt + 1) * DV], ps[:, 4 + tt, 0:DV], ACT.Square,
                                 scale=st[:, 2, tt:tt + 1], accum_out=hs[:, 0, ds(h * TT + tt, 1)]
                                 ).then_inc(sem("hsq"), 1)

            act.wait_ge(sem("gp_ok"), 1)
            keys(0)
            decay(0, range(TT))
            with act.Fori(0, MH - 1) as h:
                keys(h + 1)
                decay(h + 1, range(2))
                squares(h)
                decay(h + 1, range(2, TT))
            squares(MH - 1)
            act.wait_ge(sem("hsq"), MH * TT)
            a.activation(hs[:, 1, :], hs[:, 0, :], ACT.Sqrt, bias=epsc[:], scale=1.0 / DV).then_inc(sem("hstd"), 1)
            affine("y0", ct[:, COL["hn"]:COL["hn"] + KT], None)
            for i in range(2):
                for s in range(2):
                    cast(s, WBIG, 7 + i)
            fetch_rows(1, 1)
            resid_norm(0, "1", gs2[:, 0, 0, :], gs2[:, 0, 1, :])
            ffn(0)
            fetch_rows(2, 2)
            resid_norm(1, "2", gs2[:, 1, 0, :], gs2[:, 1, 1, :])

            b0 = PERL // 2
            for i in range(2):
                for s in range(2):
                    fetch_unit(G1_1 + i, range(4 * s, 4 * s + 4))
                    cast(s, WBIG, b0 + 1 + i)
            act.wait_ge(sem("gate_mm1"), 1)
            fb = ct[0:FH, CFG:CFG + 1]
            me(a.activation(GB["a"][0:FH, :], ps[0:FH, 4, :], ACT.Abs, bias=fb))
            me.wait()
            me(a.activation(GB["L"][0:FH, :], GB["a"][0:FH, :], ACT.Exp, scale=-1.0))
            me.wait()
            a.activation(GB["L"][0:FH, :], GB["L"][0:FH, :], ACT.Ln, bias=ones[0:FH, 0:1]).then_inc(sem("lf1"), 1)
            for gg in range(2):
                for s in range(2):
                    cast(s, WBIG, b0 + 3 + gg)
            affine("q", gs2[:, 2, 0, :], gs2[:, 2, 1, :])
            for i in range(2):
                for s in range(2):
                    fetch_unit(SC2_1 + i, range(4 * s, 4 * s + 4))
                    cast(s, WBIG, b0 + 5 + i)
            def pair(i, first):
                def exps(hh, tb):
                    m = 4 * hh + tb
                    act.wait_ge(sem("nmax"), 8 * i + m + 1)
                    if not first or hh:
                        act.wait_ge(sem("PTps"), 8 * i + m - 3)
                    a.activation(B["Pm"][:, tb, 0:(tb + 1) * P], ps[:, tb, 0:(tb + 1) * P], ACT.Exp,
                                 bias=st[:, 0, tb:tb + 1], accum_out=st[:, 1, tb:tb + 1]).then_inc(sem("Pe"), 1)

                def keep(hh, tb):
                    act.wait_ge(sem("PTps"), 8 * i + 4 * hh + tb + 1)
                    if tb == 0 and not (first and hh == 0):
                        act.wait_ge(sem("ov"), 2 * i + hh)
                    a.copy(B["PT"][:, 0:tb + 1, tb * P:(tb + 1) * P],
                           ps[:, 4 + tb % 2, 0:(tb + 1) * P].rearrange("p (s t) -> p s t", s=tb + 1)
                           ).then_inc(sem("PT"), 1)

                for hh in range(2):
                    exps(hh, 0)
                    exps(hh, 1)
                    exps(hh, 2)
                    keep(hh, 0)
                    if hh == 0:
                        a.copy(B["vst"], B["v"][:, :, ds(i * P, P)]).then_inc(sem("vst"), 1)
                    exps(hh, 3)
                    keep(hh, 1)
                    keep(hh, 2)
                    keep(hh, 3)

            pair(0, True)
            with act.Fori(1, PAIRS) as i:
                pair(i, False)
            for i in range(2):
                for s in range(2):
                    cast(s, WBIG, b0 + 7 + i)
            fetch_rows(3, 3)
            resid_norm(2, "3", gs2[:, 0, 0, :], gs2[:, 0, 1, :])
            ffn(1)
            resid_norm(3, None, None, None)

        @block.vector
        def _(dve):
            v = nc.vector
            me = Chain(dve, sem("dve_self"))
            mult, add, sub, mx = ALU.mult, ALU.add, ALU.subtract, ALU.max

            def unit(u, a_slot, chunks=range(KT)):
                for j in chunks:
                    dve.wait_ge(m_in[j % 2], 16 * (u * (KT // 2) + j // 2 + 1))
                    c = cs[:, j:j + 1]
                    dst = (acc[:, a_slot, :] if isinstance(a_slot, int)
                           else acc[:, ds(a_slot, 1), :].rearrange("p a n -> p (a n)"))
                    if j == 0:
                        ins = v.tensor_scalar(dst, m_raw[:, 0, :], c, None, mult)
                    else:
                        dve.wait_ge(m_used[(j - 1) % 2], u * (KT // 2) + (j - 1) // 2 + 1)
                        ins = v.scalar_tensor_tensor(dst, m_raw[:, j % 2, :], c, dst, mult, add)
                    ins.then_inc(m_used[j % 2], 1)

            def fin_cols(psb, u_sh, u_sc, gain, dst_g, dst_s):
                me(v.tensor_tensor(dst_s, psb[:, 0:KT], ct[:, u_sh * KT:(u_sh + 1) * KT], add))
                me(v.tensor_tensor(st[:, 6:8, :].rearrange("p a n -> p (a n)"), psb[:, KT:2 * KT],
                                   ct[:, u_sc * KT:(u_sc + 1) * KT], add))
                me.wait()
                return v.scalar_tensor_tensor(dst_g, st[:, 6:8, :].rearrange("p a n -> p (a n)"), 1.0,
                                              ct[:, COL[gain]:COL[gain] + KT], add, mult)

            def fin_gate(banks, a_slot, n):
                dve.wait_ge(rows_in, 16 * (n + 1))
                me(v.tensor_tensor(acc[:, a_slot, :], ps[:, banks:banks + 2, :].rearrange("p a n -> p (a n)"),
                                   brow[:, 0, :], add))
                me.wait()
                return v.tensor_tensor(acc[:, a_slot, :], acc[:, a_slot, :], brow[:, 1, :], mult)

            def normalise(tag, fresh=True):
                for tt in range(TT):
                    if fresh:
                        dve.wait_ge(sem(f"xstd{tag}"), tt + 1)
                        me(v.reciprocal(st[:, 5, tt:tt + 1], st[:, 4, tt:tt + 1]))
                        me.wait()
                    if tt >= 2:
                        dve.wait_ge(sem(f"tr{tag}"), tt - 1)
                    v.tensor_scalar(xt[tt % 2], x[:, tt, :], st[:, 5, tt:tt + 1], None, mult
                                    ).then_inc(sem(f"xn{tag}"), 1)

            def split(tag):
                for f in range(KT):
                    dve.wait_ge(sem(f"hb{tag}"), f + 1)
                    me(v.tensor_copy(h_hi[:, f, :], hb[:, f % 2, :]))
                    me.wait()
                    v.tensor_tensor(h_lo[:, f, :], hb[:, f % 2, :], h_hi[:, f, :].bitcast(F32), sub
                                    ).then_inc(sem(f"h{tag}"), 1)

            def update(r, gp):
                for tt in range(TT):
                    dve.wait_ge(sem(f"ystd{r}"), tt + 1)
                    me(v.reciprocal(st[:, 2, tt:tt + 1], st[:, 1, tt:tt + 1]))
                    me.wait()
                    if tt >= 2:
                        dve.wait_ge(sem(f"x_new{r}"), tt - 1)
                    v.scalar_tensor_tensor(xt[tt % 2], ps[:, 2 * tt:2 * tt + 2, :].rearrange("p a n -> p (a n)"),
                                           st[:, 2, tt:tt + 1], acc[:, gp, :], mult, mult
                                           ).then_inc(sem(f"yread{r}"), 1)
                    dve.wait_ge(sem(f"yread{r}"), tt + 1)
                    v.tensor_tensor(x[:, tt, :], x[:, tt, :], xt[tt % 2], add).then_inc(sem(f"x_new{r}"), 1)

            def resid_norm(r, tag, gp):
                update(r, gp)
                if tag is not None:
                    dve.wait_ge(sem(f"x_new{r}"), TT)
                    normalise(tag)
                    split(tag)

            def ffn(l):
                def tile(n, s):
                    dve.wait_ge(w_used[s], l * PERL // 2 + MIXBLK // 2 + n + 1 + FREE)
                    dve.wait_ge(sem(f"sg{l}"), 2 * n + s + 1)
                    v.tensor_tensor(F["act"][:, ds(2 * n + s, 1), :].rearrange("p a n -> p (a n)"),
                                    F["sg"][:, s, :], ps[:, 2 * s + 1, :], mult).then_inc(sem(f"act{l}_{s}"), 1)

                if l == 0:
                    with dve.Fori(0, 5) as i:
                        for q in range(2):
                            for s in range(2):
                                tile(2 * i + q, s)
                                unit(G2_0 + i, i, range(4 * q + 2 * s, 4 * q + 2 * s + 2))
                    for s in range(2):
                        tile(10, s)
                else:
                    with dve.Fori(0, FT // 2) as i:
                        for s in range(2):
                            tile(i, s)
                dve.wait_ge(sem(f"gp_mm{2 * l + 1}"), 1)
                fin_gate(4, (G2_0, G2_1)[l] % ACC, 2 * l + 1).then_inc(sem("gp_ok"), 1)
                if l == 0:
                    fin_cols(ps[:, 6, 0:16], KVSH, KVSC, "kv", gs2[:, 1, 0, :], gs2[:, 1, 1, :]
                             ).then_inc(sem("fin2a"), 1)
                    dve.wait_ge(sem("fin2a"), 1)
                    fin_cols(ps[:, 6, 16:32], SH1_1, SC1_1, "mix1", gs2[:, 2, 0, :], gs2[:, 2, 1, :]
                             ).then_inc(sem("fin2"), 1)
                with dve.Fori(0, FT // 2) as i:
                    for s in range(2):
                        dve.wait_ge(sem(f"act{l}_{s}"), FT // 2 + FREE)
                        dve.wait_ge(w_used[s], (l * PERL + BIG) // 2 + i + FREE)
                        src = F["act"][:, ds(2 * i + s, 1), :].rearrange("p a n -> p (a n)")
                        v.tensor_copy(F["ahi"][:, s, :], src).then_inc(sem(f"ahi{l}_{s}"), 1)
                        dve.wait_ge(sem(f"ahi{l}_{s}"), i + 1)
                        v.tensor_tensor(F["alo"][:, s, :], src, F["ahi"][:, s, :].bitcast(F32), sub
                                        ).then_inc(sem(f"alo{l}_{s}"), 1)

            dve.wait_ge(consts_in, 16)
            dve.wait_ge(sem("cs"), 1)
            unit(SH1_0, SH1_0)
            unit(SC1_0, SC1_0)
            dve.wait_ge(m_used[1], KT)
            v.engine_nop().then_inc(acc_ok, 1)
            dve.wait_ge(sem("fin_mm0"), 1)
            fin_cols(ps[:, 0, 0:16], SH1_0, SC1_0, "mix0", gsc[:], gsh[:]).then_inc(sem("fin0a"), 1)
            dve.wait_ge(sem("fin0a"), 1)
            me(v.tensor_scalar(st[0:36, 6, 0:1], ct[0:36, CMG:CMG + 1], 1.0 / CAP, None, mult)
               )
            me.wait()
            v.engine_nop().then_inc(sem("fin0"), 1)
            v.engine_nop().then_inc(sem("gb15"), 1)
            normalise("0")
            split("0")
            dve.wait_ge(sem("gw_in"), 16)
            me(v.tensor_copy(gwh[:], gwr[:]))
            me.wait()
            v.tensor_tensor(gwl[:], gwr[:], gwh[:].bitcast(F32), sub).then_inc(sem("gw_split"), 1)

            for i in range(2):
                for s in range(2):
                    unit(G1_0 + i, (G1_0 + i) % ACC, range(4 * s, 4 * s + 4))
                    n = 2 * i + s
                    dve.wait_ge(w_used[s], i + 1 + FREE)
                    v.tensor_copy(A["qk"][:, 2 * n:2 * n + 2, :], ps[:, 2 * s:2 * s + 2, :]).then_inc(sem("qk"), 1)
            me(v.memset(A["Mp"][:].bitcast(F32), 0.0))
            me(v.memset(two[:], 0.0))
            me(v.memset(hs[:], 0.0))
            me(v.tensor_copy(ones_r[:], ones[:]))
            me(v.memset(A["v"][:, :, :, DV:DV + 1], 1.0))
            me(v.memset(G["G2"][0:64, :], 0.0))
            dve.wait_ge(sem("lf"), 1)
            me.wait()
            me(v.memset(A["w4"][0:4, :], 1.0))
            me.wait()
            me(v.tensor_tensor(two[:, 0:FH], ident[:, 0:FH], ident[:, 32:32 + FH], add))
            me(v.tensor_tensor_scan(G["nB"][0:4, :], A["w4"][0:4, :], G["L"][0:4, :], 0.0, mult, add))
            me.wait()
            me(v.scalar_tensor_tensor(G["G2"][0:4, :], G["th"][0:4, :], CAP, G["nB"][0:4, :], mult, add))
            me.wait()
            me(v.tensor_tensor_scan(G["L"][0:4, :], A["w4"][0:4, :], G["G2"][0:4, :], 0.0, mult, mx))
            me.wait()
            v.tensor_tensor(A["w4"][0:4, :], G["nB"][0:4, :], G["L"][0:4, :], sub).then_inc(sem("nbm"), 1)
            dve.wait_ge(sem("nbm"), 1)
            me(v.tensor_copy(A["Mp"][0:4, :], G["L"][0:4, :]))
            me.wait()
            me(v.tensor_tensor(A["Mp"][32:36, :], G["L"][0:4, :], A["Mp"][0:4, :].bitcast(F32), sub))
            me.wait()
            for gg in range(2):
                unit(SC2_0, SC2_0 % ACC, range(4 * gg, 4 * gg + 4))
                dve.wait_ge(w_used[1], 3 + gg + FREE)
                for tt in range(TT):
                    v.tensor_copy(A["v"][:, tt, 2 * gg:2 * gg + 2, 0:DV],
                                  ps[:, 4 * (gg % 2) + tt, :].rearrange("p (h n) -> p h n", h=2)
                                  ).then_inc(sem("v"), 1)
            dve.wait_ge(sem("gt_mm"), 1)
            me(v.tensor_copy(A["gc"][:], ps[:, 3, 0:TT * 36].rearrange("p (t n) -> p t n", t=TT)))
            me.wait()
            v.engine_nop().then_inc(sem("gc"), 1)
            dve.wait_ge(sem("gp_mm0"), 1)
            fin_gate(1, G1_0 % ACC, 0).then_inc(sem("gp_ok"), 1)
            fin_cols(ps[:, 0, 0:16], SH2_0, SC2_0, "ffn0", gs2[:, 0, 0, :], gs2[:, 0, 1, :]
                     ).then_inc(sem("fin1"), 1)

            def stabiliser(h):
                if not (isinstance(h, int) and h == 0):
                    dve.wait_ge(sem("E"), h)
                v.tensor_scalar(A["Mh"][:], A["Mp"][:].bitcast(F32), two[:, ds(h, 1)], -1.0, mult, mult
                                ).then_inc(sem("Mh"), 1)

            def weigh(h):
                for sb_ in range(TT):
                    n = S - sb_ * P
                    dve.wait_ge(sem("kq"), 4 * h + sb_ + 1)
                    dve.wait_ge(sem("wT"), 4 * h + sb_ + 1)
                    v.scalar_tensor_tensor(A["sT"][:, sb_, sb_ * P:S], ps[:, 1 + sb_ % 2, 0:n], float(DK) ** -0.5,
                                           A["wT"][:, sb_ % 2, 0:n], mult, mult).then_inc(sem(f"sT_{sb_ % 2}"), 1)

            def outputs(h):
                dve.wait_ge(sem("num"), h + 1)
                den = ps[:, 4:8, DV:DV + 1].rearrange("p t o -> p (t o)")
                em = A["gc"][:, :, ds(32 + h, 1)].rearrange("p t o -> p (t o)")
                me(v.scalar_tensor_tensor(st[:, 0, :], den, -1.0, em, mult, mx))
                me.wait()
                me(v.tensor_tensor(st[:, 1, :], den, st[:, 0, :], mx))
                me.wait()
                v.reciprocal(st[:, 2, :], st[:, 1, :]).then_inc(sem("rden"), 1)
                dve.wait_ge(sem("rden"), h + 1)
                for tt in range(TT):
                    o = A["og"][:, tt, ds(h * DV, DV)]
                    dve.wait_ge(sem("hsq"), TT * h + tt + 1)
                    v.scalar_tensor_tensor(o, ps[:, 4 + tt, 0:DV], st[:, 2, tt:tt + 1], o, mult, mult
                                           ).then_inc(sem("yh"), 1)

            dve.wait_ge(sem("og"), 8)
            stabiliser(0)
            weigh(0)
            with dve.Fori(0, MH - 1) as h:
                me.loop(h, 2)
                stabiliser(h + 1)
                outputs(h)
                weigh(h + 1)
            me.end(MH - 1)
            outputs(MH - 1)
            dve.wait_ge(sem("hstd"), 1)
            me(v.reciprocal(hs[:, 0, :], hs[:, 1, :]))
            me.wait()
            dve.wait_ge(sem("yh"), MH * TT + FREE)
            for tt in range(TT):
                for h in range(MH):
                    o = A["og"][:, tt, h * DV:(h + 1) * DV]
                    v.tensor_scalar(o, o, hs[:, 0, h * TT + tt:h * TT + tt + 1], None, mult
                                    ).then_inc(sem("xny0"), 1)
            split("y0")
            resid_norm(0, "1", G1_0 % ACC)
            ffn(0)
            resid_norm(1, "2", G2_0 % ACC)

            dve.wait_ge(sem("gw_in"), 32)
            me(v.tensor_copy(gwh[:], gwr[:]))
            me.wait()
            v.tensor_tensor(gwl[:], gwr[:], gwh[:].bitcast(F32), sub).then_inc(sem("gw_split"), 1)
            for i in range(2):
                for s in range(2):
                    unit(G1_1 + i, i, range(4 * s, 4 * s + 4))
                    n = 2 * i + s
                    dve.wait_ge(w_used[s], PERL // 2 + i + 1 + FREE)
                    v.tensor_copy(B["k"][:, 2 * n:2 * n + 2, :], ps[:, 2 * s:2 * s + 2, :]).then_inc(sem("k"), 1)
            me(v.memset(B["nF"][:].bitcast(F32), 0.0))
            dve.wait_ge(sem("lf1"), 1)
            me(v.tensor_scalar(GB["mn"][0:FH, :], ps[0:FH, 4, :], ct[0:FH, CFG:CFG + 1], 0.0, add, ALU.min))
            me.wait()
            me(v.tensor_tensor(GB["L"][0:FH, :], GB["L"][0:FH, :], GB["mn"][0:FH, :], sub))
            me(v.memset(GB["a"][0:FH, :], 1.0))
            me.wait()
            me(v.tensor_tensor_scan(GB["F"][0:FH, :], GB["a"][0:FH, :], GB["L"][0:FH, :], 0.0, mult, add))
            me.wait()
            me(v.tensor_copy(B["nF"][0:FH, :], GB["F"][0:FH, :]))
            me.wait()
            v.tensor_tensor(B["nF"][32:32 + FH, :], GB["F"][0:FH, :], B["nF"][0:FH, :].bitcast(F32), sub
                            ).then_inc(sem("nF"), 1)
            for gg in range(2):
                dve.wait_ge(w_used[1], PERL // 2 + 3 + gg + FREE)
                for tt in range(TT):
                    v.tensor_copy(B["v"][:, tt, gg * HALF:(gg + 1) * HALF], ps[:, 4 * (gg % 2) + tt, :]
                                  ).then_inc(sem("v1"), 1)
            normalise("q", fresh=False)
            split("q")
            for i in range(2):
                for s in range(2):
                    unit(SC2_1 + i, 2 + i, range(4 * s, 4 * s + 4))
                    n = 2 * i + s
                    dve.wait_ge(w_used[s], PERL // 2 + 4 + i + 1 + FREE)
                    v.tensor_scalar(B["q"][:, 2 * n:2 * n + 2, :], ps[:, 2 * s:2 * s + 2, :], float(HD) ** -0.5,
                                    None, mult).then_inc(sem("q"), 1)
            dve.wait_ge(sem("gp_mm2"), 1)
            fin_gate(0, G1_1 % ACC, 2).then_inc(sem("gp_ok"), 1)
            fin_cols(ps[:, 2, 0:16], SH2_1, SC2_1, "ffn1", gs2[:, 0, 0, :], gs2[:, 0, 1, :]
                     ).then_inc(sem("fin3"), 1)
            dve.wait_ge(m_used[1], UNITS * KT // 2)
            me(v.tensor_copy(h_hi[:], B["k"][:]))
            me(v.memset(B["qhi"][:].bitcast(F32), 0.0))
            me(v.memset(B["qlo"][:].bitcast(F32), 0.0))
            me(v.memset(hb[:, 1, :], 0.0))
            me.wait()
            v.engine_nop().then_inc(sem("k_hi"), 1)
            v.engine_nop().then_inc(sem("qst0"), 1)
            dve.wait_ge(sem("nF"), 1)

            def pair_queries(i):
                dve.wait_ge(sem("q"), 4)
                if not (isinstance(i, int) and i == 0):
                    dve.wait_ge(sem("qlo"), 2 * i)
                v.tensor_copy(hb[:, 0, :], B["q"][:, ds(i, 1), :].rearrange("p a n -> p (a n)")
                              ).then_inc(sem("qs"), 1)

            def decay_row(head):
                v.tensor_scalar(B["nFm"][:, head[1], :], B["nF"][:].bitcast(F32), two[:, ds(head[0], 1)], None, mult
                                ).then_inc(sem("nFm"), 1)

            def output(i, hh):
                dve.wait_ge(sem("ov"), 2 * i + hh + 1)
                r = slice(64 * hh, 64 * hh + 64)
                v.tensor_copy(B["q"][r, ds(i, 1), :].rearrange("p a n -> p (a n)"), ps[r, 6 + hh, :]
                              ).then_inc(sem("oc"), 1)

            def pair(i, first, last=False):
                def top(hh, tb):
                    dve.wait_ge(sem("S_mm"), 8 * i + 4 * hh + tb + 1)
                    v.tensor_reduce(st[:, 0, tb:tb + 1], ps[:, tb, 0:(tb + 1) * P], AX_X, mx, negate=True
                                    ).then_inc(sem("nmax"), 1)

                def scale(hh, tb):
                    dve.wait_ge(sem("Pe"), 8 * i + 4 * hh + tb + 1)
                    me(v.reciprocal(st[:, 2, tb:tb + 1], st[:, 1, tb:tb + 1]))
                    me.wait()
                    v.tensor_scalar(B["Pm"][:, tb, 0:(tb + 1) * P], B["Pm"][:, tb, 0:(tb + 1) * P],
                                    st[:, 2, tb:tb + 1], None, mult).then_inc(sem("Pn"), 1)

                for hh in range(2):
                    top(hh, 0)
                    decay_row((2 * i + hh + 1, 1 - hh))
                    if hh == 0 and not last:
                        pair_queries(i + 1)
                    top(hh, 1)
                    scale(hh, 0)
                    top(hh, 2)
                    scale(hh, 1)
                    top(hh, 3)
                    if hh == 1:
                        output(i, 0)
                    elif not first:
                        output(i - 1, 1)
                    scale(hh, 2)
                    scale(hh, 3)

            decay_row((0, 0))
            pair_queries(0)
            pair(0, True)
            with dve.Fori(1, PAIRS - 1) as i:
                me.loop(i, 8, 1)
                pair(i, False)
            me.end(PAIRS - 2)
            pair(PAIRS - 1, False, True)
            output(PAIRS - 1, 1)
            dve.wait_ge(sem("oc"), FH)
            for f in range(KT):
                me(v.tensor_copy(h_hi[:, f, :], B["q"][:, f, :]))
                me.wait()
                v.tensor_tensor(h_lo[:, f, :], B["q"][:, f, :], h_hi[:, f, :].bitcast(F32), sub
                                ).then_inc(sem("o"), 1)
            resid_norm(2, "3", G1_1 % ACC)
            ffn(1)
            resid_norm(3, None, G2_1 % ACC)

        @block.tensor
        def _(pe):
            t = nc.tensor

            def parts(order, s):
                pe.wait_ge(whi_ok[s], order + 1 + FREE)
                pe.wait_ge(wlo_ok[s], order + 1 + FREE)

            def three(dst, l_hi, l_lo, r_hi, r_lo, start, stop):
                t.matmul(dst, l_hi, r_lo, start=start, stop=False)
                t.matmul(dst, l_lo, r_hi, start=False, stop=False)
                return t.matmul(dst, l_hi, r_hi, start=False, stop=stop)

            def features(order, s, bank, arriving=None):
                parts(order, s)
                whi = w_hi[:, s, :].rearrange("p (k n) -> p k n", k=KT)
                wlo = w_lo[:, s, :].rearrange("p (k n) -> p k n", k=KT)
                for m in range(2):
                    for k in range(KT):
                        if arriving is not None and m == 0:
                            pe.wait_ge(sem(f"h{arriving}"), k + 1)
                        last = three(ps[:, bank + m, :], whi[:, k, m * P:(m + 1) * P], wlo[:, k, m * P:(m + 1) * P],
                                     h_hi[:, k, :], h_lo[:, k, :], k == 0, k == KT - 1)
                last.then_inc(w_used[s], 1)

            def tokens(order, bank):
                for s in range(2):
                    parts(order, s)
                    whi = w_hi[:, s, :].rearrange("p (k n) -> p k n", k=4)
                    wlo = w_lo[:, s, :].rearrange("p (k n) -> p k n", k=4)
                    for tt in range(TT):
                        for k4 in range(4):
                            k = 4 * s + k4
                            c = slice(tt * P, (tt + 1) * P)
                            last = three(ps[:, bank + tt, :], h_hi[:, k, c], h_lo[:, k, c], whi[:, k4, :],
                                         wlo[:, k4, :], k == 0, k == KT - 1)
                    last.then_inc(w_used[s], 1)

            def adaln_cols(bank, col, unit):
                for f in range(KT):
                    last = t.matmul(ps[:, bank, col + f:col + f + 1], acc[:, unit % ACC, f * P:(f + 1) * P],
                                    ones[:, 0:1], start=True, stop=True)
                return last

            def adaln_row(bank, unit):
                for half in range(2):
                    last = t.matmul(ps[:, bank + half, :], ones[:], acc[:, unit % ACC, half * HALF:(half + 1) * HALF],
                                    start=True, stop=True)
                return last

            def transpose(tag, src=None):
                for tt in range(TT):
                    pe.wait_ge(sem(f"xn{tag}"), tt + 1 if src is None else MH * (tt + 1))
                    for k in range(KT):
                        tile = xt[tt % 2] if src is None else src[:, tt, :]
                        last = t.transpose(ps[:, k, tt * P:(tt + 1) * P], tile[:, k * P:(k + 1) * P], ident[:])
                    last.then_inc(sem(f"tr{tag}"), 1)

            def gate_mm(m, done):
                for k in range(KT):
                    last = three(ps[0:m, 4, :], gwh[:, k, 0:m], gwl[:, k, 0:m], h_hi[:, k, :], h_lo[:, k, :],
                                 k == 0, k == KT - 1)
                last.then_inc(done, 1)

            def out_proj(order, r, arriving):
                for g in range(2):
                    for s in range(2):
                        parts(order + g, s)
                        whi = w_hi[:, s, :].rearrange("p (k n) -> p k n", k=4)
                        wlo = w_lo[:, s, :].rearrange("p (k n) -> p k n", k=4)
                        for tt in range(TT):
                            for k4 in range(4):
                                k = 4 * s + k4
                                c = slice(tt * P, (tt + 1) * P)
                                if g == 0:
                                    pe.wait_ge(arriving, max(k, 2 * tt + (tt > 0)) + 1)
                                last = three(ps[:, 2 * tt + g, :], h_hi[:, k, c], h_lo[:, k, c], whi[:, k4, :],
                                             wlo[:, k4, :], k == 0, k == KT - 1)
                            if g == 1 and s == 1:
                                last.then_inc(sem(f"y{r}"), 1)
                        if g == 0 or s == 0:
                            last.then_inc(w_used[s], 1)
                last_used(1, f"y{r}")

            def last_used(s, y):
                pe.wait_ge(sem(y), TT)
                pe.sem_inc(w_used[s], 1)

            def ffn(l):
                base = l * PERL // 2 + MIXBLK // 2
                down = (l * PERL + BIG) // 2
                r = 2 * l + 1
                with pe.Fori(0, FT // 2) as i:
                    for s in range(2):
                        parts(base + i, s)
                        pe.wait_ge(sem(f"act{l}_{s}"), i + FREE)
                        whi = w_hi[:, s, :].rearrange("p (k n) -> p k n", k=KT)
                        wlo = w_lo[:, s, :].rearrange("p (k n) -> p k n", k=KT)
                        for m in range(2):
                            for k in range(KT):
                                if s == 0 and m == 0:
                                    pe.wait_ge(sem(f"h{r}"), k + 1)
                                last = three(ps[:, 2 * s + m, :], whi[:, k, m * P:(m + 1) * P],
                                             wlo[:, k, m * P:(m + 1) * P], h_hi[:, k, :], h_lo[:, k, :],
                                             k == 0, k == KT - 1)
                            if m == 0:
                                last.then_inc(sem(f"g{l}"), 1)
                        last.then_inc(w_used[s], 1)
                pe.wait_ge(m_used[1], ((SC1_1, G2_1)[l] + 1) * KT // 2)
                last = adaln_row(4, (G2_0, G2_1)[l])
                if l == 0:
                    for n, u in enumerate((KVSH, KVSC, SH1_1, SC1_1)):
                        last = adaln_cols(6, KT * n, u)
                last.then_inc(sem(f"gp_mm{r}"), 1)
                for s in range(2):
                    pe.wait_ge(sem(f"act{l}_{s}"), FT // 2 + FREE)
                pe.wait_ge(sem("gp_ok"), 2 * l + 2)
                if l == 0:
                    pe.wait_ge(sem("fin2"), 1)

                def ktile(i, s, start, stop):
                    parts(down + i, s)
                    pe.wait_ge(sem(f"alo{l}_{s}"), i + 1)
                    for tt in range(TT):
                        c = slice(tt * P, (tt + 1) * P)
                        for half in range(2):
                            n = slice(half * HALF, (half + 1) * HALF)
                            last = three(ps[:, 2 * tt + half, :], F["ahi"][:, s, c], F["alo"][:, s, c],
                                         w_hi[:, s, n], w_lo[:, s, n], start, stop)
                        if stop:
                            last.then_inc(sem(f"y{r}"), 1)
                    if not stop:
                        last.then_inc(w_used[s], 1)

                ktile(0, 0, True, False)
                ktile(0, 1, False, False)
                with pe.Fori(1, FT // 2 - 1) as i:
                    for s in range(2):
                        ktile(i, s, False, False)
                ktile(FT // 2 - 1, 0, False, False)
                ktile(FT // 2 - 1, 1, False, True)
                last_used(1, f"y{r}")

            pe.wait_ge(acc_ok, 1)
            pe.wait_ge(setup_pool, 1)
            adaln_cols(0, 0, SH1_0)
            adaln_cols(0, KT, SC1_0).then_inc(sem("fin_mm0"), 1)
            pe.wait_ge(sem("fin0"), 1)
            transpose("0")
            for i in range(2):
                for s in range(2):
                    n = 2 * i + s
                    if i:
                        pe.wait_ge(sem("qk"), n - 1)
                    features(i, s, 2 * s, "0" if i + s == 0 else None)
            pe.wait_ge(sem("gw_split"), 1)
            gate_mm(36, sem("gate_mm0"))
            pe.wait_ge(sem("qk"), 4)
            tokens(2, 0)
            pe.wait_ge(sem("lf"), 1)
            tokens(3, 4)
            pe.wait_ge(sem("v"), 4)
            tokens(4, 0)
            pe.wait_ge(sem("v"), 8)
            tokens(5, 4)
            pe.wait_ge(sem("og"), 4)
            pe.wait_ge(sem("em"), 1)
            for tt in range(TT):
                last = t.transpose(ps[:, 3, tt * 36:(tt + 1) * 36], G["G2"][0:36, tt * P:(tt + 1) * P],
                                   ident[0:36, 0:36])
            last.then_inc(sem("gt_mm"), 1)
            pe.wait_ge(sem("og"), 8)
            pe.wait_ge(sem("gc"), 1)
            adaln_row(1, G1_0)
            adaln_cols(0, 0, SH2_0)
            adaln_cols(0, KT, SC2_0).then_inc(sem("gp_mm0"), 1)
            pe.wait_ge(sem("gp_ok"), 1)
            pe.wait_ge(sem("fin1"), 1)

            def decay(h):
                pe.wait_ge(sem("Mh"), h + 1)
                if not (isinstance(h, int) and h == 0):
                    pe.wait_ge(sem("wT"), 4 * h)
                t.matmul(ps[:, 0, :], ones_r[:], A["Mh"][:], start=True, stop=True)
                t.matmul(ps[:, 3, :], ones_r[:], A["Mh"][:], start=True, stop=False)
                for tb in range(TT):
                    last = t.matmul(ps[:, 3, tb * P:(tb + 1) * P], identb[:], trib[:, 0, :], start=False,
                                    stop=tb == TT - 1)
                last.then_inc(sem("E"), 1)

            def key_query(h, tiles):
                pe.wait_ge(sem("kst"), h + 1)
                for sb_ in tiles:
                    q = A["qk"][:, ds(h, 1), :].rearrange("p a n -> p (a n)")[:, sb_ * P:S]
                    if not (isinstance(h, int) and h == 0 and sb_ < 2):
                        pe.wait_ge(sem(f"sT_{sb_ % 2}"), 2 * h + sb_ // 2)
                    t.matmul(ps[:, 1 + sb_ % 2, 0:S - sb_ * P], A["kst"][:, sb_ * P:(sb_ + 1) * P], q,
                             start=True, stop=True).then_inc(sem("kq"), 1)

            def numerator(h):
                for p_ in range(2):
                    pe.wait_ge(sem(f"sT_{p_}"), 2 * h + 2)
                pe.wait_ge(sem("yh"), 4 * h + FREE)
                for tt in range(TT):
                    for sb_ in range(tt + 1):
                        last = t.matmul(ps[:, 4 + tt, 0:DV + 1], A["sT"][:, sb_, tt * P:(tt + 1) * P],
                                        A["v"][:, sb_, ds(h, 1), :].rearrange("p a n -> p (a n)"),
                                        start=sb_ == 0, stop=sb_ == tt)
                last.then_inc(sem("num"), 1)

            decay(0)
            key_query(0, range(2))
            with pe.Fori(0, MH - 1) as h:
                key_query(h, range(2, TT))
                decay(h + 1)
                key_query(h + 1, range(2))
                numerator(h)
            key_query(MH - 1, range(2, TT))
            numerator(MH - 1)
            pe.wait_ge(sem("yh"), MH * TT + FREE)
            transpose("y0", A["og"])
            out_proj(6, 0, sem("hy0"))
            pe.wait_ge(sem("yread0"), TT)
            transpose("1")
            ffn(0)
            pe.wait_ge(sem("yread1"), TT)
            transpose("2")

            b0 = PERL // 2
            for i in range(2):
                for s in range(2):
                    if i:
                        pe.wait_ge(sem("k"), 2 * i + s - 1)
                    features(b0 + i, s, 2 * s, "2" if i + s == 0 else None)
            pe.wait_ge(sem("gw_split"), 2)
            gate_mm(FH, sem("gate_mm1"))
            pe.wait_ge(sem("k"), 4)
            tokens(b0 + 2, 0)
            pe.wait_ge(sem("nF"), 1)
            tokens(b0 + 3, 4)
            pe.wait_ge(sem("v1"), 8)
            transpose("q")
            for i in range(2):
                for s in range(2):
                    if i:
                        pe.wait_ge(sem("q"), 2 * i + s - 1)
                    features(b0 + 4 + i, s, 2 * s, "q" if i + s == 0 else None)
            pe.wait_ge(sem("q"), 4)
            adaln_row(0, G1_1)
            adaln_cols(2, 0, SH2_1)
            adaln_cols(2, KT, SC2_1).then_inc(sem("gp_mm2"), 1)
            pe.wait_ge(sem("fin3"), 1)
            pe.wait_ge(sem("gp_ok"), 3)

            def scores(pair, hh, tb, first=False):
                n = (tb + 1) * P
                c = slice(tb * P, n)
                khi = h_hi[:, ds(pair, 1), :].rearrange("p a n -> p (a n)")[:, 0:n]
                klo = h_lo[:, ds(pair, 1), :].rearrange("p a n -> p (a n)")[:, 0:n]
                if tb == 0:
                    pe.wait_ge(sem("k_lo"), 1 if isinstance(pair, int) and pair == 0 else 2)
                    pe.wait_ge(sem("qlo"), 2 * pair + hh + 1)
                    pe.wait_ge(sem("nFm"), 2 * pair + hh + 1)
                if not first:
                    pe.wait_ge(sem("Pe"), 8 * pair + 4 * hh + tb - 3)
                t.matmul(ps[:, tb, 0:n], B["qhi"][:, hh, c], klo, start=True, stop=False)
                t.matmul(ps[:, tb, 0:n], B["qlo"][:, hh, c], khi, start=False, stop=False)
                t.matmul(ps[:, tb, 0:n], B["qhi"][:, hh, c], khi, start=False, stop=False)
                t.matmul(ps[:, tb, 0:n], ones_r[:], B["nFm"][:, hh, 0:n], start=False, stop=False)
                t.matmul(ps[:, tb, n - P:n], identb[:], trib[:, 1, :], start=False, stop=True
                         ).then_inc(sem("S_mm"), 1)

            def pair(i, first, last_pair):
                for hh in range(2):
                    for tb in range(TT):
                        m = 4 * hh + tb
                        pe.wait_ge(sem("Pn"), 8 * i + m + 1)
                        if not first or m >= 2:
                            pe.wait_ge(sem("PT"), 8 * i + m - 1)
                        for sb_ in range(tb + 1):
                            last = t.transpose(ps[:, 4 + tb % 2, sb_ * P:(sb_ + 1) * P],
                                               B["Pm"][:, tb, sb_ * P:(sb_ + 1) * P], ident[:])
                        last.then_inc(sem("PTps"), 1)
                        if hh == 0:
                            scores(i, 1, tb)
                        elif not last_pair:
                            scores(i + 1, 0, tb)
                    pe.wait_ge(sem("vst"), i + 1)
                    pe.wait_ge(sem("PT"), 8 * i + 4 * hh + 4)
                    if not first:
                        pe.wait_ge(sem("oc"), 2 * i + hh - 1)
                    for sb_ in range(TT):
                        last = t.matmul(ps[:, 6 + hh, sb_ * P:S], B["vst"][:, sb_, :], B["PT"][:, sb_, sb_ * P:S],
                                        start=sb_ == 0, stop=sb_ == TT - 1)
                    last.then_inc(sem("ov"), 1)

            for tb in range(TT):
                scores(0, 0, tb, first=True)
            pair(0, True, False)
            with pe.Fori(1, PAIRS - 1) as i:
                pair(i, False, False)
            pair(PAIRS - 1, False, True)
            out_proj(b0 + 6, 2, sem("o"))
            pe.wait_ge(sem("yread2"), TT)
            transpose("3")
            ffn(1)


_SHAPE = (1, S, D)


def lay_out(a):
    f = np.float32

    def feat(w):
        n = w.shape[1] // (2 * P)
        return w.reshape(KT, P, n, 2 * P).transpose(2, 1, 0, 3).reshape(n, P, WBIG)

    def tok(w):
        n = w.shape[1] // HALF
        return w.reshape(2, 4, P, n, HALF).transpose(3, 0, 2, 1, 4).reshape(2 * n, P, WBIG)

    def up(w):
        return w.reshape(KT, P, 2, FT, P).transpose(3, 1, 0, 2, 4).reshape(FT, P, WBIG)

    aw, kw = a["a_w_in"][0], a["kv_w"]
    big = np.concatenate([
        feat(aw[:, :D]), tok(aw[:, D:3 * D]), tok(a["a_w_out"][0]), up(a["ffn_w_in"][0]),
        feat(kw[:, :D]), tok(kw[:, D:2 * D]), feat(a["b_w_q"][0]), tok(a["b_w_out"][0]), up(a["ffn_w_in"][1])])
    small = a["ffn_w_out"].reshape(2 * FT, P, D)
    order = [(0, 0), (0, 1), (0, 2), (0, 3), (0, 4), (0, 5), "k0", "k1", (1, 0), (1, 1), (1, 2), (1, 3), (1, 4), (1, 5)]
    mats, bias = [], []
    for o in order:
        m, b = (a["kv_mod_w"], a["kv_mod_b"]) if isinstance(o, str) else (a["mod_w"][o[0]], a["mod_b"][o[0]])
        j = int(o[1])
        mats.append(m[:, j * D:(j + 1) * D].reshape(KT, P, D))
        bias.append(b[j * D:(j + 1) * D])
    mods = np.concatenate(mats)
    gains = [a["mix_pre_g"][0], a["ffn_pre_g"][0], a["kv_norm_g"], a["mix_pre_g"][1], a["ffn_pre_g"][1],
             a["a_hnorm_g"][0], a["c"][0]]
    cols = np.zeros((P, NCOL), f)
    for i, vec in enumerate(bias + gains):
        cols[:, i * KT:(i + 1) * KT] = vec.reshape(KT, P).T
    cols[0:4, CMG] = a["a_gate_b"][0][:4]
    cols[32:36, CMG] = a["a_gate_b"][0][4:]
    cols[0:FH, CFG] = a["kv_fgate_b"]
    rows = np.stack([np.stack([bias[G1_0], a["mix_post_g"][0]]), np.stack([bias[G2_0], a["ffn_post_g"][0]]),
                     np.stack([bias[G1_1], a["mix_post_g"][1]]), np.stack([bias[G2_1], a["ffn_post_g"][1]])])
    gw0 = np.zeros((P, KT, 36), f)
    gate = aw[:, 3 * D:].reshape(KT, P, 2 * MH).transpose(1, 0, 2)
    gw0[:, :, 0:4], gw0[:, :, 32:36] = gate[:, :, :4], gate[:, :, 4:]
    gw1 = np.zeros((P, KT, 36), f)
    gw1[:, :, 0:FH] = kw[:, 2 * D:].reshape(KT, P, FH).transpose(1, 0, 2)
    return {"x_in": a["x"][0], "wbig": big, "wsmall": small, "mods": mods, "cols": cols, "rows": rows,
            "gw0": gw0, "gw1": gw1}


def kernel(**inputs):
    import concourse.bacc as bacc
    from concourse.bass_utils import run_bass_kernel_spmd

    arrays = {n: np.ascontiguousarray(v) for n, v in
              lay_out({n: np.asarray(v) for n, v in inputs.items()}).items()}
    nc = bacc.Bacc("TRN2", target_bir_lowering=False, num_devices=1)
    aps = [nc.dram_tensor(f"in_{n}", v.shape, F32, kind="ExternalInput").ap() for n, v in arrays.items()]
    out = nc.dram_tensor("out_y", (S, D), F32, kind="ExternalOutput").ap()
    build(nc, *aps, out)
    r = run_bass_kernel_spmd(nc, [{f"in_{n}": v for n, v in arrays.items()}], core_ids=[0])
    return r.results[0]["out_y"].reshape(_SHAPE)
```

```python
from contextlib import ExitStack

import numpy as np

import concourse.bass as bass
from concourse import mybir

F32 = mybir.dt.float32
F32R = mybir.dt.float32r
BF16 = mybir.dt.bfloat16
ALU = mybir.AluOpType
ACT = mybir.ActivationFunctionType
AX_X = mybir.AxisListType.X
ds = bass.ds

P = 128
D = 1024
S = 512
KT = D // P
TT = S // P
HALF = 512
MH = 4
DK = D // (2 * MH)
DV = D // MH
DVX = DV + 2
FH = 16
HD = D // FH
PAIRS = FH // 2
FF = 2816
FT = FF // P
CAP = 15.0
EPS = 1e-6
WBIG = 2 * D
WSMALL = D
MIXBLK = 16
BIG = MIXBLK + FT
PERL = BIG + FT
UNITS = 14
NEG = -1.0e30
FREE = 1
(SH1_0, SC1_0, G1_0, SH2_0, SC2_0, G2_0, KVSH, KVSC, SH1_1, SC1_1, G1_1, SH2_1, SC2_1, G2_1) = range(UNITS)
POOL_ADDS = [(1,), (0, 2), (1,), (0, 1)]
SQUARES = ["y0 y1 x0 y2 x1 y3 x2 x3", "y0 y1 y2 x0 y3 x1 x2 x3"]
UPDATES = ["u0 u1 n0 u2 n1 u3 n2 n3", "u0 u1 u2 n0 u3 n1 n2 n3"]
PRE = 14
ACC = 5
GAINS = ["mix0", "ffn0", "kv", "mix1", "ffn1", "hn", "c"]
CB = UNITS * KT
COL = {n: CB + i * KT for i, n in enumerate(GAINS)}
CMG = CB + len(GAINS) * KT
CFG = CMG + 1
NCOL = CFG + 1


class Chain:

    def __init__(self, eng, sem):
        self.eng, self.sem = eng, sem
        self.base, self.k, self.i, self.per, self.start = 0, 0, None, 0, 0

    def loop(self, i, per, start=0):
        self.base, self.i, self.per, self.k = self.base + self.k - start * per, i, per, 0
        self.start = start

    def end(self, trips):
        assert self.k == self.per, (self.k, self.per)
        self.base, self.i, self.k, self.per = self.base + (trips + self.start) * self.per, None, 0, 0

    def __call__(self, ins):
        self.k += 1
        ins.then_inc(self.sem, 1)
        return ins

    def wait(self):
        n = self.base + self.k
        self.eng.wait_ge(self.sem, n if self.i is None else self.i * self.per + n)


def turn(u, j):
    return u * (KT // 2) + j // 2 - PRE // 2


def build(nc, x_in, wbig, wsmall, mods, cols, rows, gw0, gw1, out):
    ctx = ExitStack()
    with ctx:
        def sb(name, shape, dt=F32):
            return ctx.enter_context(nc.sbuf_tensor(name, shape, dt))

        sems = {}

        def sem(name):
            if name not in sems:
                sems[name] = ctx.enter_context(nc.semaphore(name))
            return sems[name]

        x = sb("x", [P, TT, D])
        h_at = nc.sbuf_base
        h_hi = sb("h_hi", [P, KT, S], F32R)
        h_lo = sb("h_lo", [P, KT, S], F32R)
        w_raw = sb("w_raw", [P, 2, WBIG])
        w_hi = sb("w_hi", [P, 2, WBIG], F32R)
        w_lo = sb("w_lo", [P, 2, WBIG], F32R)
        m_at = nc.sbuf_base
        m_raw = sb("m_raw", [P, 2, D])
        acc = sb("acc", [P, ACC, D])
        brow = sb("brow", [P, 2, D])
        xn = sb("xn", [P, D])
        junk = sb("junk", [P, D], BF16)
        ct = sb("ct", [P, NCOL])
        cs = sb("cs", [P, KT])
        norms = sb("norms", [P, 5, 2, KT])
        st = sb("st", [P, 8, TT])
        ident = sb("ident", [P, P])
        ones = sb("ones", [P, P])
        ones_r = sb("ones_r", [P, P], F32R)
        two = sb("two", [P, FH + 4])
        hs = sb("hs", [P, 2, MH * TT])
        identb = sb("identb", [P, P], BF16)
        trib = sb("trib", [P, 2, P], BF16)
        epsc = sb("epsc", [P, 1])
        gwr = sb("gwr", [P, KT, 36])
        gwh = sb("gwh", [P, KT, 36], F32R)
        gwl = sb("gwl", [P, KT, 36], F32R)
        hb = sb("hb", [P, 2, HALF])
        norm = {n: (norms[:, i, 0, :], norms[:, i, 1, :]) for i, n in enumerate(GAINS[:5])}
        xt = [xn[:], hb[:].rearrange("p a n -> p (a n)")]

        a0 = (nc.sbuf_base + 31) // 32 * 32
        room = nc.sbuf_usable_end - a0

        def place(tag, want):
            at, got = a0, {}
            for name, shape, dt in want:
                size = int(np.prod(shape[1:])) * (2 if dt == BF16 else 4)
                got[name] = nc.alloc_sbuf_tensor_at(f"{tag}_{name}", shape, dt, offset=at)
                at += (size + 31) // 32 * 32
            assert at - a0 <= room, (tag, at - a0, room)
            return got

        A = place("a", [("qk", [P, 8, S], F32), ("v", [P, TT, MH, DVX], F32), ("og", [P, TT, D], F32),
                        ("sT", [P, TT, S], F32R), ("Mp", [P, S], F32R), ("gc", [P, TT, 36], F32)])
        acc_at = m_at + 2 * D * 4
        A["wT"] = acc[:, 0, :].rearrange("p (a n) -> p a n", a=2)
        A["kst"], A["w4"] = acc[:, 1, 0:S], acc[:, 1, S:2 * S]
        A["Mh"] = nc.alloc_sbuf_tensor_at("a_Mh", [P, S], F32R, offset=acc_at + (D + S) * 4)
        A["vlo"] = nc.alloc_sbuf_tensor_at("a_vlo", [P, TT, MH, DVX], F32R, offset=a0 + 8 * S * 4)
        A["vhi"] = nc.alloc_sbuf_tensor_at("a_vhi", [P, TT, MH, DVX], F32R, offset=h_at)
        A["sTlo"] = nc.alloc_sbuf_tensor_at("a_sTlo", [P, TT, S], F32R, offset=h_at + TT * MH * DVX * 4)
        off = a0 + (8 * S + TT * MH * DVX + TT * D) * 4
        G = {}
        for i, name in enumerate(["th", "L", "nB", "G2"]):
            G[name] = nc.alloc_sbuf_tensor_at(f"g_{name}", [P, S], F32, offset=off + i * S * 4)
        B = place("b", [("k", [P, PAIRS, S], F32), ("v", [P, TT, D], F32), ("q", [P, PAIRS, S], F32),
                        ("PT", [P, TT, S], F32), ("nF", [P, S], F32R)])
        B["qhi"] = nc.alloc_sbuf_tensor_at("b_qhi", [P, 2, S], F32R, offset=m_at)
        B["qlo"] = nc.alloc_sbuf_tensor_at("b_qlo", [P, 2, S], F32R, offset=m_at + D * 4)
        B["nFm"] = nc.alloc_sbuf_tensor_at("b_nFm", [P, 2, S], F32R, offset=acc_at + 4 * D * 4)
        nq = [xn[:], acc[:, 3, :], acc[:, 4, :], B["PT"][:, 0:2, :].rearrange("p a n -> p (a n)")]
        B["Pm"] = brow[:].rearrange("p a (b n) -> p (a b) n", b=2)
        B["vst"] = xn[:, 0:TT * P].rearrange("p (a n) -> p a n", a=TT)
        off = a0 + (PAIRS * S + TT * D + PAIRS * S) * 4
        GB = {}
        for i, name in enumerate(["a", "mn", "L", "F"]):
            GB[name] = nc.alloc_sbuf_tensor_at(f"gb_{name}", [P, S], F32, offset=off + i * S * 4)
        pre = nc.alloc_sbuf_tensor_at("pre", [P, PRE, D], F32, offset=a0)
        nx_all = nc.alloc_sbuf_tensor_at("nx", [P, TT, D], F32, offset=a0)
        nx = [nx_all[:, tt, :] for tt in range(TT)]
        F = place("f", [("act", [P, FT, S], F32), ("sg", [P, 2, S], F32), ("ahi", [P, 2, S], F32R),
                        ("alo", [P, 2, S], F32R)])

        ps = ctx.enter_context(nc.psum_tensor("ps", [P, 8, HALF], F32))

        w_in = [sem("w_in0"), sem("w_in1")]
        whi_ok = [sem("whi_ok0"), sem("whi_ok1")]
        wlo_ok = [sem("wlo_ok0"), sem("wlo_ok1")]
        w_used = [sem("w_used0"), sem("w_used1")]
        m_in = [sem("m_in0"), sem("m_in1")]
        m_used = [sem("m_used0"), sem("m_used1")]
        acc_ok = sem("acc_ok")
        consts_in, rows_in, x_in_ok = sem("consts_in"), sem("rows_in"), sem("x_in_ok")
        setup_pool = sem("setup_pool")

        def updated(r, tt):
            own = [n for n in range(TT) if (n in POOL_ADDS[r]) == (tt in POOL_ADDS[r])]
            return sem(f"x_{'pool' if tt in POOL_ADDS[r] else 'dve'}{r}"), own.index(tt) + 1

        block = ctx.enter_context(nc.Block())

        @block.sync
        def _(sp):
            sp.dma_start(ct[:], cols).then_inc(consts_in, 16)
            for one in whi_ok + wlo_ok + w_used:
                sp.sem_inc(one, FREE)
            for name in ("act0_0", "act0_1", "act1_0", "act1_1"):
                sp.sem_inc(sem(name), FREE)
            sp.sem_inc(sem("yh"), TT)
            for tt in range(TT):
                sp.dma_start(x[:, tt, :], x_in[tt * P:(tt + 1) * P, :]).then_inc(x_in_ok, 16)

            def load(src, width, index, slot, order):
                sp.wait_ge(whi_ok[slot], order + FREE)
                sp.wait_ge(wlo_ok[slot], order + FREE)
                sp.dma_start(w_raw[:, slot, 0:width],
                             src[ds(index, 1)].rearrange("a p n -> p (a n)")).then_inc(w_in[slot], 16)

            def first_chunks(group):
                c = slice(4 * group, min(4 * group + 4, PRE))
                sp.dma_start(pre[:, c, :], mods[c].rearrange("a p n -> p a n")).then_inc(sem(f"pre{group}"), 16)

            for group in range(2):
                first_chunks(group)
            load(wbig, WBIG, 0, 0, 0)
            for group in range(2, 4):
                first_chunks(group)
            for slot in range(2):
                sp.dma_start(m_raw[:, slot, :], mods[PRE + slot]).then_inc(m_in[slot], 16)
            load(wbig, WBIG, 1, 1, 0)
            sp.dma_start(gwr[:], gw0).then_inc(sem("gw_in"), 16)

            for l in range(2):
                if l == 1:
                    sp.wait_ge(sem("gw_split"), 1)
                    sp.dma_start(gwr[:], gw1).then_inc(sem("gw_in"), 16)
                with sp.Fori(0 if l else 1, BIG // 2) as i:
                    for s in range(2):
                        load(wbig, WBIG, l * BIG + 2 * i + s, s, l * PERL // 2 + i)
                with sp.Fori(0, FT // 2) as i:
                    for s in range(2):
                        load(wsmall, WSMALL, l * FT + 2 * i + s, s, (l * PERL + BIG) // 2 + i)
            for tt in range(TT):
                sp.wait_ge(*updated(3, tt))
                sp.dma_start(out[tt * P:(tt + 1) * P, :], x[:, tt, :]).then_inc(sem("stored"), 16)
            sp.wait_ge(sem("stored"), 16 * TT)

        @block.gpsimd
        def _(pool):
            g = nc.gpsimd
            chain = Chain(pool, sem("pool_self"))
            chain(g.memset(ident[:], 0.0))
            chain(g.memset(identb[:], 0.0))
            chain(g.memset(trib[:], 0.0))
            chain(g.memset(ones[:], 1.0))
            chain(g.memset(epsc[:], EPS))
            chain.wait()
            for m in (ident, identb):
                chain(g.affine_select(out=m[:], in_=m[:], compare_op=ALU.not_equal, fill=1.0, base=0,
                                      pattern=[[-1, P]], channel_multiplier=1))
            chain(g.affine_select(out=trib[:, 0, :], in_=trib[:, 0, :], compare_op=ALU.is_ge, fill=NEG, base=0,
                                  pattern=[[1, P]], channel_multiplier=-1))
            chain(g.affine_select(out=trib[:, 1, :], in_=trib[:, 1, :], compare_op=ALU.is_ge, fill=NEG, base=0,
                                  pattern=[[-1, P]], channel_multiplier=1))
            chain.wait()
            g.engine_nop().then_inc(setup_pool, 1)

            def split(slot, width, order):
                pool.wait_ge(whi_ok[slot], order + 1 + FREE)
                pool.wait_ge(w_used[slot], order + FREE)
                g.tensor_tensor(w_lo[:, slot, 0:width], w_raw[:, slot, 0:width],
                                w_hi[:, slot, 0:width].bitcast(F32), ALU.subtract).then_inc(wlo_ok[slot], 1)

            def splits(width, first, end):
                with pool.Fori(first, end) as order:
                    for s in range(2):
                        split(s, width, order)

            def boundary(r, order):
                if r % 2 == 0:
                    split(0, WBIG, order)
                for tt in POOL_ADDS[r]:
                    pool.wait_ge(sem(f"yread{r}"), tt + 1)
                    g.tensor_tensor(x[:, tt, :], x[:, tt, :], xt[tt % 2], ALU.add).then_inc(updated(r, tt)[0], 1)
                if r == 1:
                    split(0, WBIG, order)
                if order is not None:
                    split(1, WBIG, order)

            for l in range(2):
                b0 = l * PERL // 2
                ffn_in = b0 + MIXBLK // 2
                splits(WBIG, b0 + (1 if l else 0), ffn_in - 2)
                split(0, WBIG, ffn_in - 2)
                if l == 0:
                    def values(h):
                        pool.wait_ge(sem("vhi"), h + 1)
                        g.tensor_tensor(A["vlo"][:, :, h, :], A["v"][:, :, h, :],
                                        A["vhi"][:, :, h, :].bitcast(F32), ALU.subtract).then_inc(sem("vlo"), 1)

                    def scores(h, sb_):
                        pool.wait_ge(sem("sThi"), 4 * h + sb_ + 1)
                        c = slice(sb_ * P, S)
                        g.tensor_tensor(A["sTlo"][:, sb_, c], hb[:, sb_ % 2, c],
                                        A["sT"][:, sb_, c].bitcast(F32), ALU.subtract).then_inc(sem("sTlo"), 1)

                    values(0)
                    scores(0, 0)
                    scores(0, 1)
                    values(1)
                    scores(0, 2)
                    scores(0, 3)
                    split(1, WBIG, ffn_in - 2)
                    values(2)
                    values(3)
                    with pool.Fori(1, MH) as h:
                        for sb_ in range(TT):
                            scores(h, sb_)
                if l == 1:
                    def queries(i, hh, first):
                        r = slice(64 * hh, 64 * hh + 64)
                        pool.wait_ge(sem("qs"), i + 1)
                        if not first:
                            pool.wait_ge(sem("S_mm"), 8 * i - 4 + 4 * hh)
                            pool.wait_ge(sem("qlo"), 2 * i + hh)
                        g.tensor_tensor(B["qhi"][r, hh, :], hb[r, 0, :], hb[r, 1, :], ALU.add).then_inc(sem("qhi"), 1)
                        pool.wait_ge(sem("qhi"), 2 * i + hh + 1)
                        g.tensor_tensor(B["qlo"][r, hh, :], hb[r, 0, :], B["qhi"][r, hh, :].bitcast(F32),
                                        ALU.subtract).then_inc(sem("qlo"), 1)

                    def keys(pairs, done):
                        pool.wait_ge(sem("k_hi"), done)
                        g.tensor_tensor(h_lo[:, pairs, :], B["k"][:, pairs, :], h_hi[:, pairs, :].bitcast(F32),
                                        ALU.subtract).then_inc(sem("k_lo"), 1)

                    pool.wait_ge(sem("q_room"), 1)
                    queries(0, 0, True)
                    pool.wait_ge(sem("qlo"), 1)
                    queries(0, 1, True)
                    pool.wait_ge(sem("qlo"), 2)
                    keys(slice(0, 1), 1)
                    keys(slice(1, PAIRS), 2)
                    split(1, WBIG, ffn_in - 2)
                    pool.wait_ge(sem("k_lo"), 2)
                    with pool.Fori(1, PAIRS) as i:
                        for hh in range(2):
                            queries(i, hh, False)
                    pool.wait_ge(sem("qlo"), FH)
                for s in range(2):
                    split(s, WBIG, ffn_in - 1)
                boundary(2 * l, ffn_in)
                splits(WBIG, ffn_in + 1, b0 + BIG // 2)
                splits(WSMALL, b0 + BIG // 2, b0 + PERL // 2)
                boundary(2 * l + 1, None if l else PERL // 2)

        @block.scalar
        def _(act):
            a = nc.scalar
            me = Chain(act, sem("act_self"))

            def cast(slot, width, order):
                act.wait_ge(w_in[slot], 16 * (order + 1))
                act.wait_ge(w_used[slot], order + FREE)
                a.copy(w_hi[:, slot, 0:width], w_raw[:, slot, 0:width]).then_inc(whi_ok[slot], 1)

            def fetch(index, slot, order):
                act.wait_ge(m_used[slot], order)
                act.dma_start(m_raw[:, slot, :], mods[ds(index, 1)].rearrange("a p n -> p (a n)")
                              ).then_inc(m_in[slot], 16)

            def fetch_unit(u, chunks=range(KT)):
                for j in chunks:
                    if u * KT + j + 2 >= UNITS * KT:
                        break
                    fetch(u * KT + j + 2, j % 2, turn(u, j) + 1)

            def fetch_rows(n, before):
                if before:
                    act.wait_ge(sem("gp_ok"), before)
                act.dma_start(brow[:], rows[n].partition_broadcast(P)).then_inc(rows_in, 16)

            def square_sum(src, col, tt, n, sem_std):
                me(a.activation(junk[:, 0:D], src, ACT.Square, accum_out=st[:, col, tt:tt + 1]))
                me.wait()
                a.activation(st[:, col + 1, tt:tt + 1], st[:, col, tt:tt + 1], ACT.Sqrt, bias=epsc[:],
                             scale=1.0 / n).then_inc(sem_std, 1)

            def affine(tag, scale, shift, late=None):
                for f in range(KT):
                    act.wait_ge(sem(f"tr{tag}"), {"y0": f // 2 + 1, "q": f + 1, "0": TT - 1 + KT}.get(tag, TT + f))
                    if f >= 2:
                        act.wait_ge(sem(f"h{tag}"), f - 1)
                    src = xn[:, 0:S] if tag == "0" and f == KT - 1 else ps[:, f, :]
                    a.activation(hb[:, f % 2, :], src, ACT.Identity, scale=scale[:, f:f + 1],
                                 bias=(shift[:, f:f + 1] if shift is not None else 0.0)
                                 ).then_inc(sem(f"hb{tag}"), 1)
                    if late is not None and f == 3:
                        cast(1, WBIG, late)

            def rms_table():
                me(a.activation(st[:, 6, 0:1], epsc[:], ACT.Sqrt))

            def resid_norm(r, tag, scale, shift, late=None, early=None):
                for step in SQUARES[r % 2].split():
                    kind, tt = step[0], int(step[1])
                    if kind == "y":
                        act.wait_ge(sem(f"y{r}"), tt + 1)
                        square_sum(ps[:, 2 * tt:2 * tt + 2, :], 0, tt, D, sem(f"ystd{r}"))
                    elif tag is not None:
                        act.wait_ge(*updated(r, tt))
                        square_sum(x[:, tt, :], 3, tt, D, sem(f"xstd{tag}"))
                    if step == "x2" and early is not None:
                        cast(0, WBIG, early)
                if tag is not None:
                    affine(tag, scale, shift, late)

            def ffn(l):
                base = l * PERL // 2 + MIXBLK // 2
                down = (l * PERL + BIG) // 2

                def tile(n, s, width):
                    act.wait_ge(sem(f"g{l}"), 2 * n + s + 1)
                    act.wait_ge(sem(f"act{l}_{s}"), n + FREE)
                    a.activation(F["sg"][:, s, :], ps[:, 2 * s, :], ACT.Silu).then_inc(sem(f"sg{l}"), 1)
                    cast(s, width, base + n + 1)

                if l == 0:
                    with act.Fori(0, 5) as i:
                        for q in range(2):
                            for s in range(2):
                                tile(2 * i + q, s, WBIG)
                                for j in range(4 * q + 2 * s, 4 * q + 2 * s + 2):
                                    fetch((G2_0 + i) * KT + j + 2, j % 2, turn(G2_0 + i, j) + 1)
                    for s in range(2):
                        tile(10, s, WSMALL)
                else:
                    for i in range(2):
                        for s in range(2):
                            tile(i, s, WBIG)
                            fetch_unit(G2_1, range(4 * i + 2 * s, 4 * i + 2 * s + 2))
                    with act.Fori(2, FT // 2 - 1) as i:
                        for s in range(2):
                            tile(i, s, WBIG)
                    for s in range(2):
                        tile(FT // 2 - 1, s, WSMALL)
                with act.Fori(0, FT // 2 - 1) as i:
                    for s in range(2):
                        cast(s, WSMALL, down + i + 1)
                rms_table()

            act.wait_ge(consts_in, 16)
            a.activation(cs[:], ct[:, COL["c"]:COL["c"] + KT], ACT.Silu).then_inc(sem("cs"), 1)
            act.wait_ge(setup_pool, 1)
            act.wait_ge(x_in_ok, 16 * TT)
            for tt in range(TT):
                square_sum(x[:, tt, :], 3, tt, D, sem("xstd0"))
            cast(0, WBIG, 0)
            fetch_unit(SC1_0, range(KT - 2, KT))
            act.wait_ge(sem("fin0"), 1)
            affine("0", *norm["mix0"], 0)
            fetch_rows(0, 0)

            for i in range(2):
                for s in range(2):
                    cast(s, WBIG, i + 1)
                    fetch_unit(G1_0 + i, range(4 * s, 4 * s + 4))
            act.wait_ge(sem("gate_mm0"), 1)
            act.wait_ge(sem("gb15"), 1)
            me(a.activation(G["th"][0:36, :], ps[0:36, 4, :], ACT.Tanh, scale=1.0 / CAP, bias=st[0:36, 6, 0:1]))
            me.wait()
            me(a.activation(G["L"][0:4, :], G["th"][32:36, :], ACT.Exp, scale=-CAP))
            me.wait()
            a.activation(G["L"][0:4, :], G["L"][0:4, :], ACT.Ln, bias=ones[0:4, 0:1]).then_inc(sem("lf"), 1)
            act.wait_ge(sem("nbm"), 1)
            a.activation(G["G2"][32:36, :], A["w4"][0:4, :], ACT.Exp).then_inc(sem("em"), 1)
            for gg in range(4):
                for s in range(2):
                    cast(s, WBIG, 3 + gg)
                    if gg < 2:
                        fetch_unit(SC2_0, range(4 * gg + 2 * s, 4 * gg + 2 * s + 2))
                if gg >= 2:
                    act.wait_ge(w_used[1], 3 + gg + FREE)
                    for tt in range(TT):
                        a.activation(A["og"][:, tt, (gg - 2) * HALF:(gg - 1) * HALF], ps[:, 4 * (gg % 2) + tt, :],
                                     ACT.Sigmoid).then_inc(sem("og"), 1)
            def keys(h):
                if not (isinstance(h, int) and h == 0):
                    act.wait_ge(sem("kq"), 4 * h)
                a.copy(A["kst"], A["qk"][:, ds(MH + h, 1), :].rearrange("p a n -> p (a n)")
                       ).then_inc(sem("kst"), 1)

            def decay(h):
                act.wait_ge(sem("E"), h + 1)
                for sb_ in range(TT):
                    if not (isinstance(h, int) and h == 0 and sb_ < 2):
                        act.wait_ge(sem(f"sT_{sb_ % 2}"), 2 * h + sb_ // 2)
                    last = a.activation(A["wT"][:, sb_ % 2, 0:P], ps[:, 3, sb_ * P:(sb_ + 1) * P], ACT.Exp,
                                        bias=A["gc"][:, sb_, ds(h, 1)])
                    if sb_ < TT - 1:
                        last = a.activation(A["wT"][:, sb_ % 2, P:S - sb_ * P], ps[:, 0, (sb_ + 1) * P:S], ACT.Exp,
                                            bias=A["gc"][:, sb_, ds(h, 1)])
                    last.then_inc(sem("wT"), 1)

            def squares(h):
                act.wait_ge(sem("rden"), h + 1)
                for tt in range(TT):
                    a.activation(junk[:, tt * DV:(tt + 1) * DV], ps[:, 4 + tt, 0:DV], ACT.Square,
                                 scale=st[:, 2, tt:tt + 1], accum_out=hs[:, 0, ds(h * TT + tt, 1)]
                                 ).then_inc(sem("hsq"), 1)

            keys(0)
            decay(0)
            keys(1)
            with act.Fori(0, MH - 2) as h:
                decay(h + 1)
                keys(h + 2)
                squares(h)
            decay(MH - 1)
            squares(MH - 2)
            def head_rms(first, end):
                act.wait_ge(sem("hsq"), end * TT)
                c = slice(first * TT, end * TT)
                a.activation(hs[:, 1, c], hs[:, 0, c], ACT.Sqrt, bias=epsc[:], scale=1.0 / DV
                             ).then_inc(sem("hstd"), 1)

            head_rms(0, MH - 1)
            squares(MH - 1)
            head_rms(MH - 1, MH)
            affine("y0", ct[:, COL["hn"]:COL["hn"] + KT], None)
            for order, s in ((7, 0), (7, 1), (8, 0)):
                cast(s, WBIG, order)
            fetch_rows(1, 1)
            resid_norm(0, "1", *norm["ffn0"], MIXBLK // 2)
            ffn(0)
            fetch_rows(2, 2)
            resid_norm(1, "2", *norm["kv"], PERL // 2, PERL // 2)

            b0 = PERL // 2
            for i in range(2):
                for s in range(2):
                    cast(s, WBIG, b0 + 1 + i)
                    fetch_unit(G1_1 + i, range(4 * s, 4 * s + 4))
            act.wait_ge(sem("gate_mm1"), 1)
            fb = ct[0:FH, CFG:CFG + 1]
            me(a.activation(GB["a"][0:FH, :], ps[0:FH, 4, :], ACT.Abs, bias=fb))
            me.wait()
            me(a.activation(GB["L"][0:FH, :], GB["a"][0:FH, :], ACT.Exp, scale=-1.0))
            me.wait()
            a.activation(GB["L"][0:FH, :], GB["L"][0:FH, :], ACT.Ln, bias=ones[0:FH, 0:1]).then_inc(sem("lf1"), 1)
            for gg in range(2):
                for s in range(2):
                    cast(s, WBIG, b0 + 3 + gg)
            affine("q", *norm["mix1"])
            for i in range(2):
                for s in range(2):
                    cast(s, WBIG, b0 + 5 + i)
                    if i == 0:
                        fetch_unit(SC2_1, range(4 * s, (4, KT - 2)[s]))

            def pair(i, first):
                def exps(hh, tb):
                    m = 4 * hh + tb
                    act.wait_ge(sem("nmax"), 8 * i + m + 1)
                    if not first or hh:
                        act.wait_ge(sem("PTps"), 8 * i + m - 3)
                    a.activation(B["Pm"][:, tb, 0:(tb + 1) * P], ps[:, tb, 0:(tb + 1) * P], ACT.Exp,
                                 bias=st[:, 0, tb:tb + 1], accum_out=st[:, 1, tb:tb + 1]).then_inc(sem("Pe"), 1)

                def keep(hh, tb):
                    act.wait_ge(sem("PTps"), 8 * i + 4 * hh + tb + 1)
                    if tb == 0 and not (first and hh == 0):
                        act.wait_ge(sem("ov"), 2 * i + hh)
                    a.copy(B["PT"][:, 0:tb + 1, tb * P:(tb + 1) * P],
                           ps[:, 4 + tb % 2, 0:(tb + 1) * P].rearrange("p (s t) -> p s t", s=tb + 1)
                           ).then_inc(sem("PT"), 1)

                for hh in range(2):
                    exps(hh, 0)
                    exps(hh, 1)
                    exps(hh, 2)
                    keep(hh, 0)
                    if hh == 0:
                        a.copy(B["vst"], B["v"][:, :, ds(i * P, P)]).then_inc(sem("vst"), 1)
                    exps(hh, 3)
                    keep(hh, 1)
                    keep(hh, 2)
                    keep(hh, 3)

            act.wait_ge(sem("gp_ok"), 3)
            pair(0, True)
            with act.Fori(1, PAIRS) as i:
                pair(i, False)
            act.wait_ge(sem("S_mm"), 8 * PAIRS)
            fetch_unit(SC2_1, range(KT - 2, KT))
            rms_table()
            for order, s in ((b0 + 7, 0), (b0 + 7, 1), (b0 + 8, 0)):
                cast(s, WBIG, order)
            fetch_rows(3, 3)
            resid_norm(2, "3", *norm["ffn1"], b0 + MIXBLK // 2)
            ffn(1)
            resid_norm(3, None, None, None)

        @block.vector
        def _(dve):
            v = nc.vector
            me = Chain(dve, sem("dve_self"))
            mult, add, sub, mx = ALU.mult, ALU.add, ALU.subtract, ALU.max

            def unit(u, a_slot, chunks=range(KT)):
                for j in chunks:
                    early = isinstance(u, int) and u * KT + j < PRE
                    if early:
                        dve.wait_ge(sem(f"pre{(u * KT + j) // 4}"), 16)
                        src = pre[:, u * KT + j, :]
                    else:
                        dve.wait_ge(m_in[j % 2], 16 * (turn(u, j) + 1))
                        src = m_raw[:, j % 2, :]
                    c = cs[:, j:j + 1]
                    dst = (acc[:, a_slot, :] if isinstance(a_slot, int)
                           else acc[:, ds(a_slot, 1), :].rearrange("p a n -> p (a n)"))
                    if j == 0:
                        ins = v.tensor_scalar(dst, src, c, None, mult)
                    else:
                        if isinstance(u, int) and u * KT + j <= PRE:
                            me.wait()
                        else:
                            dve.wait_ge(m_used[(j - 1) % 2], turn(u, j - 1) + 1)
                        ins = v.scalar_tensor_tensor(dst, src, c, dst, mult, add)
                    if early:
                        me(ins)
                    else:
                        ins.then_inc(m_used[j % 2], 1)

            def fin_cols(psb, u_sh, u_sc, gain):
                dst_g, dst_s = norm[gain]
                me(v.tensor_tensor(dst_s, psb[:, 0:KT], ct[:, u_sh * KT:(u_sh + 1) * KT], add))
                me(v.tensor_tensor(st[:, 6:8, :].rearrange("p a n -> p (a n)"), psb[:, KT:2 * KT],
                                   ct[:, u_sc * KT:(u_sc + 1) * KT], add))
                me.wait()
                return v.scalar_tensor_tensor(dst_g, st[:, 6:8, :].rearrange("p a n -> p (a n)"), 1.0,
                                              ct[:, COL[gain]:COL[gain] + KT], add, mult)

            def fin_gate(banks, a_slot, n):
                dve.wait_ge(rows_in, 16 * (n + 1))
                me(v.tensor_tensor(acc[:, a_slot, :], ps[:, banks:banks + 2, :].rearrange("p a n -> p (a n)"),
                                   brow[:, 0, :], add))
                me.wait()
                return v.tensor_tensor(acc[:, a_slot, :], acc[:, a_slot, :], brow[:, 1, :], mult)

            def normalise(tag, tiles, dst, fresh=True):
                for tt in tiles:
                    if fresh:
                        dve.wait_ge(sem(f"xstd{tag}"), tt + 1)
                        me(v.reciprocal(st[:, 5, tt:tt + 1], st[:, 4, tt:tt + 1]))
                        me.wait()
                    if tt >= len(dst):
                        dve.wait_ge(sem(f"tr{tag}"), tt + 1 - len(dst))
                    v.tensor_scalar(dst[tt % len(dst)], x[:, tt, :], st[:, 5, tt:tt + 1], None, mult
                                    ).then_inc(sem(f"xn{tag}"), 1)

            def split(tag):
                for f in range(KT):
                    dve.wait_ge(sem(f"hb{tag}"), f + 1)
                    me(v.tensor_copy(h_hi[:, f, :], hb[:, f % 2, :]))
                    me.wait()
                    v.tensor_tensor(h_lo[:, f, :], hb[:, f % 2, :], h_hi[:, f, :].bitcast(F32), sub
                                    ).then_inc(sem(f"h{tag}"), 1)

            def resid_norm(r, tag, gp):
                def update(tt):
                    dve.wait_ge(sem(f"ystd{r}"), tt + 1)
                    me(v.reciprocal(st[:, 2, tt:tt + 1], st[:, 1, tt:tt + 1]))
                    me.wait()
                    if tt >= 2:
                        dve.wait_ge(*updated(r, tt - 2))
                    v.scalar_tensor_tensor(xt[tt % 2], ps[:, 2 * tt:2 * tt + 2, :].rearrange("p a n -> p (a n)"),
                                           st[:, 2, tt:tt + 1], acc[:, gp, :], mult, mult
                                           ).then_inc(sem(f"yread{r}"), 1)
                    if tt not in POOL_ADDS[r]:
                        dve.wait_ge(sem(f"yread{r}"), tt + 1)
                        v.tensor_tensor(x[:, tt, :], x[:, tt, :], xt[tt % 2], add).then_inc(updated(r, tt)[0], 1)

                for step in UPDATES[r % 2].split():
                    if step[0] == "u":
                        update(int(step[1]))
                    elif tag is not None:
                        normalise(tag, [int(step[1])], nx)
                if tag is not None:
                    split(tag)

            def ffn(l):
                def tile(n, s):
                    dve.wait_ge(w_used[s], l * PERL // 2 + MIXBLK // 2 + n + 1 + FREE)
                    dve.wait_ge(sem(f"sg{l}"), 2 * n + s + 1)
                    v.tensor_tensor(F["act"][:, ds(2 * n + s, 1), :].rearrange("p a n -> p (a n)"),
                                    F["sg"][:, s, :], ps[:, 2 * s + 1, :], mult).then_inc(sem(f"act{l}_{s}"), 1)

                if l == 0:
                    with dve.Fori(0, 5) as i:
                        for q in range(2):
                            for s in range(2):
                                tile(2 * i + q, s)
                                unit(G2_0 + i, i, range(4 * q + 2 * s, 4 * q + 2 * s + 2))
                else:
                    for i in range(2):
                        for s in range(2):
                            tile(i, s)
                            unit(G2_1, G2_1 % ACC, range(4 * i + 2 * s, 4 * i + 2 * s + 2))
                    with dve.Fori(2, FT // 2 - 1) as i:
                        for s in range(2):
                            tile(i, s)
                def parts(i, s, first):
                    dve.wait_ge(sem(f"act{l}_{s}"), (1 if first else FT // 2) + FREE)
                    if not first:
                        dve.wait_ge(w_used[s], (l * PERL + BIG) // 2 + i + FREE)
                    src = F["act"][:, ds(2 * i + s, 1), :].rearrange("p a n -> p (a n)")
                    v.tensor_copy(F["ahi"][:, s, :], src).then_inc(sem(f"ahi{l}_{s}"), 1)
                    dve.wait_ge(sem(f"ahi{l}_{s}"), i + 1)
                    v.tensor_tensor(F["alo"][:, s, :], src, F["ahi"][:, s, :].bitcast(F32), sub
                                    ).then_inc(sem(f"alo{l}_{s}"), 1)

                for s in range(2):
                    parts(0, s, True)
                tile(FT // 2 - 1, 0)
                dve.wait_ge(sem(f"gp_mm{2 * l + 1}"), 1)
                fin_gate(4, (G2_0, G2_1)[l] % ACC, 2 * l + 1).then_inc(sem("gp_ok"), 1)
                if l == 0:
                    fin_cols(ps[:, 6, 0:16], KVSH, KVSC, "kv"
                             ).then_inc(sem("fin2a"), 1)
                    dve.wait_ge(sem("fin2a"), 1)
                    fin_cols(ps[:, 6, 16:32], SH1_1, SC1_1, "mix1"
                             ).then_inc(sem("fin2"), 1)
                tile(FT // 2 - 1, 1)
                with dve.Fori(1, FT // 2) as i:
                    for s in range(2):
                        parts(i, s, False)

            dve.wait_ge(consts_in, 16)
            dve.wait_ge(sem("cs"), 1)
            normalise("0", range(TT), xt)
            unit(SH1_0, SH1_0, range(4))
            dve.wait_ge(sem("tr0"), TT - 1 + KT)
            v.tensor_copy(xn[:, 0:S], ps[:, KT - 1, :]).then_inc(sem("room"), 1)
            unit(SH1_0, SH1_0, range(4, KT))
            me.wait()
            v.engine_nop().then_inc(acc_ok, 1)
            unit(SC1_0, SC1_0)
            dve.wait_ge(sem("fin_mm0"), 1)
            fin_cols(ps[:, KT - 1, 0:16], SH1_0, SC1_0, "mix0").then_inc(sem("fin0"), 1)
            dve.wait_ge(sem("fin0"), 1)
            v.tensor_scalar(st[0:36, 6, 0:1], ct[0:36, CMG:CMG + 1], 1.0 / CAP, None, mult).then_inc(sem("gb15"), 1)
            split("0")
            dve.wait_ge(sem("gw_in"), 16)
            me(v.tensor_copy(gwh[:], gwr[:]))
            me.wait()
            v.tensor_tensor(gwl[:], gwr[:], gwh[:].bitcast(F32), sub).then_inc(sem("gw_split"), 1)

            for i in range(2):
                for s in range(2):
                    n = 2 * i + s
                    dve.wait_ge(w_used[s], i + 1 + FREE)
                    v.tensor_copy(A["qk"][:, 2 * n:2 * n + 2, :], ps[:, 2 * s:2 * s + 2, :]).then_inc(sem("qk"), 1)
                    unit(G1_0 + i, (G1_0 + i) % ACC, range(4 * s, 4 * s + 4))
            me(v.memset(A["Mp"][:].bitcast(F32), 0.0))
            me(v.memset(two[:], 0.0))
            me(v.memset(hs[:], 0.0))
            me(v.tensor_copy(ones_r[:], ones[:]))
            me(v.memset(A["v"][:, :, :, DV:DVX], 1.0))
            me(v.memset(G["G2"][0:64, :], 0.0))
            dve.wait_ge(sem("lf"), 1)
            me.wait()
            me(v.memset(A["w4"][0:4, :], 1.0))
            me.wait()
            me(v.tensor_tensor(two[:, 0:FH], ident[:, 0:FH], ident[:, 32:32 + FH], add))
            me(v.tensor_tensor_scan(G["nB"][0:4, :], A["w4"][0:4, :], G["L"][0:4, :], 0.0, mult, add))
            me.wait()
            me(v.scalar_tensor_tensor(G["G2"][0:4, :], G["th"][0:4, :], CAP, G["nB"][0:4, :], mult, add))
            me.wait()
            me(v.tensor_tensor_scan(G["L"][0:4, :], A["w4"][0:4, :], G["G2"][0:4, :], 0.0, mult, mx))
            me.wait()
            v.tensor_tensor(A["w4"][0:4, :], G["nB"][0:4, :], G["L"][0:4, :], sub).then_inc(sem("nbm"), 1)
            dve.wait_ge(sem("nbm"), 1)
            me(v.tensor_copy(A["Mp"][0:4, :], G["L"][0:4, :]))
            me.wait()
            me(v.tensor_tensor(A["Mp"][32:36, :], G["L"][0:4, :], A["Mp"][0:4, :].bitcast(F32), sub))
            me.wait()
            for gg in range(2):
                unit(SC2_0, SC2_0 % ACC, range(4 * gg, 4 * gg + 2))
                dve.wait_ge(w_used[1], 3 + gg + FREE)
                for tt in range(TT):
                    v.tensor_copy(A["v"][:, tt, 2 * gg:2 * gg + 2, 0:DV],
                                  ps[:, 4 * (gg % 2) + tt, :].rearrange("p (h n) -> p h n", h=2)
                                  ).then_inc(sem("v"), 1)
                unit(SC2_0, SC2_0 % ACC, range(4 * gg + 2, 4 * gg + 4))
            dve.wait_ge(sem("gt_mm"), 1)
            me(v.tensor_copy(A["gc"][:], ps[:, 3, 0:TT * 36].rearrange("p (t n) -> p t n", t=TT)))
            me.wait()
            v.engine_nop().then_inc(sem("gc"), 1)

            def stabiliser(h):
                if not (isinstance(h, int) and h == 0):
                    dve.wait_ge(sem("E"), h)
                v.tensor_scalar(A["Mh"][:], A["Mp"][:].bitcast(F32), two[:, ds(h, 1)], -1.0, mult, mult
                                ).then_inc(sem("Mh"), 1)

            def weigh(h, tiles):
                for sb_ in tiles:
                    n = S - sb_ * P
                    c = slice(sb_ * P, S)
                    dve.wait_ge(sem("kq"), 4 * h + sb_ + 1)
                    dve.wait_ge(sem("wT"), 4 * h + sb_ + 1)
                    head0 = isinstance(h, int) and h == 0
                    if not (head0 and sb_ < 2):
                        dve.wait_ge(sem("sTlo"), 4 * h + sb_ - 1)
                    v.scalar_tensor_tensor(hb[:, sb_ % 2, c], ps[:, 1 + sb_ % 2, 0:n], float(DK) ** -0.5,
                                           A["wT"][:, sb_ % 2, 0:n], mult, mult).then_inc(sem(f"sT_{sb_ % 2}"), 1)
                    dve.wait_ge(sem(f"sT_{sb_ % 2}"), 2 * h + sb_ // 2 + 1)
                    if not head0:
                        dve.wait_ge(sem("sT_used"), 4 * h + sb_ - 3)
                    v.tensor_copy(A["sT"][:, sb_, c], hb[:, sb_ % 2, c]).then_inc(sem("sThi"), 1)

            def denominators(h):
                dve.wait_ge(sem("sT_used"), 4 * h + 4)
                den = ps[:, 4:8, DV:DV + 1].rearrange("p t o -> p (t o)")
                em = A["gc"][:, :, ds(32 + h, 1)].rearrange("p t o -> p (t o)")
                me(v.scalar_tensor_tensor(st[:, 0, :], den, -1.0, em, mult, mx))
                me.wait()
                me(v.tensor_tensor(st[:, 1, :], den, st[:, 0, :], mx))
                me.wait()
                v.reciprocal(st[:, 2, :], st[:, 1, :]).then_inc(sem("rden"), 1)

            def outputs(h):
                dve.wait_ge(sem("rden"), h + 1)
                for tt in range(TT):
                    o = A["og"][:, tt, ds(h * DV, DV)]
                    dve.wait_ge(sem("hsq"), TT * h + tt + 1)
                    v.scalar_tensor_tensor(o, ps[:, 4 + tt, 0:DV], st[:, 2, tt:tt + 1], o, mult, mult
                                           ).then_inc(sem("yh"), 1)

            def rms_scale(first, end, done):
                dve.wait_ge(sem("hstd"), done)
                c = slice(first * TT, end * TT)
                me(v.reciprocal(hs[:, 0, c], hs[:, 1, c]))
                me.wait()
                dve.wait_ge(sem("yh"), (end + 1) * TT)
                for h in range(first, end):
                    for tt in range(TT):
                        o = A["og"][:, tt, h * DV:(h + 1) * DV]
                        v.tensor_scalar(o, o, hs[:, 0, h * TT + tt:h * TT + tt + 1], None, mult
                                        ).then_inc(sem("xny0"), 1)

            stabiliser(0)
            dve.wait_ge(sem("og"), 8)
            v.tensor_copy(A["vhi"][:, :, 0, :], A["v"][:, :, 0, :]).then_inc(sem("vhi"), 1)
            weigh(0, range(2))
            stabiliser(1)
            for h in range(1, MH):
                v.tensor_copy(A["vhi"][:, :, h, :], A["v"][:, :, h, :]).then_inc(sem("vhi"), 1)
            weigh(0, range(2, TT))
            dve.wait_ge(sem("row_mm0"), 1)
            fin_gate(4, G1_0 % ACC, 0).then_inc(sem("gp_ok"), 1)
            dve.wait_ge(sem("gp_mm0"), 1)
            fin_cols(ps[:, 6, 0:16], SH2_0, SC2_0, "ffn0"
                     ).then_inc(sem("fin1"), 1)
            with dve.Fori(0, MH - 1) as h:
                me.loop(h, 2)
                weigh(h + 1, range(2))
                stabiliser(h + 2)
                weigh(h + 1, range(2, 3))
                denominators(h)
                weigh(h + 1, range(3, TT))
                outputs(h)
            me.end(MH - 1)
            rms_scale(0, MH - 1, 1)
            denominators(MH - 1)
            outputs(MH - 1)
            rms_scale(MH - 1, MH, 2)
            split("y0")
            resid_norm(0, "1", G1_0 % ACC)
            ffn(0)
            resid_norm(1, "2", G2_0 % ACC)

            dve.wait_ge(sem("gw_in"), 32)
            me(v.tensor_copy(gwh[:], gwr[:]))
            me.wait()
            v.tensor_tensor(gwl[:], gwr[:], gwh[:].bitcast(F32), sub).then_inc(sem("gw_split"), 1)
            for i in range(2):
                for s in range(2):
                    n = 2 * i + s
                    dve.wait_ge(w_used[s], PERL // 2 + i + 1 + FREE)
                    v.tensor_copy(B["k"][:, 2 * n:2 * n + 2, :], ps[:, 2 * s:2 * s + 2, :]).then_inc(sem("k"), 1)
                    unit(G1_1 + i, i, range(4 * s, 4 * s + 4))
            me(v.memset(B["nF"][:].bitcast(F32), 0.0))
            dve.wait_ge(sem("lf1"), 1)
            me(v.tensor_scalar(GB["mn"][0:FH, :], ps[0:FH, 4, :], ct[0:FH, CFG:CFG + 1], 0.0, add, ALU.min))
            me.wait()
            me(v.tensor_tensor(GB["L"][0:FH, :], GB["L"][0:FH, :], GB["mn"][0:FH, :], sub))
            me(v.memset(GB["a"][0:FH, :], 1.0))
            me.wait()
            me(v.tensor_tensor_scan(GB["F"][0:FH, :], GB["a"][0:FH, :], GB["L"][0:FH, :], 0.0, mult, add))
            me.wait()
            me(v.tensor_copy(B["nF"][0:FH, :], GB["F"][0:FH, :]))
            me.wait()
            v.tensor_tensor(B["nF"][32:32 + FH, :], GB["F"][0:FH, :], B["nF"][0:FH, :].bitcast(F32), sub
                            ).then_inc(sem("nF"), 1)
            for gg in range(2):
                if gg == 1:
                    normalise("q", range(TT), nq, fresh=False)
                dve.wait_ge(w_used[1], PERL // 2 + 3 + gg + FREE)
                for tt in range(TT):
                    v.tensor_copy(B["v"][:, tt, gg * HALF:(gg + 1) * HALF], ps[:, 4 * (gg % 2) + tt, :]
                                  ).then_inc(sem("v1"), 1)
            split("q")

            def pair_queries(i):
                if isinstance(i, int) and i == 0:
                    dve.wait_ge(sem("q"), 1)
                    dve.wait_ge(sem("hq"), KT)
                else:
                    dve.wait_ge(sem("q"), 4)
                    dve.wait_ge(sem("qlo"), 2 * i)
                v.tensor_copy(hb[:, 0, :], B["q"][:, ds(i, 1), :].rearrange("p a n -> p (a n)")
                              ).then_inc(sem("qs"), 1)

            for i in range(2):
                for s in range(2):
                    n = 2 * i + s
                    dve.wait_ge(w_used[s], PERL // 2 + 4 + i + 1 + FREE)
                    if n == 3:
                        v.tensor_copy(h_hi[:, 0:1, :], B["k"][:, 0:1, :]).then_inc(sem("k_hi"), 1)
                    v.tensor_scalar(B["q"][:, 2 * n:2 * n + 2, :], ps[:, 2 * s:2 * s + 2, :], float(HD) ** -0.5,
                                    None, mult).then_inc(sem("q"), 1)
                    if i == 0:
                        unit(SC2_1, SC2_1 % ACC, range(4 * s, 4 * s + 4))
                    if n == 2:
                        dve.wait_ge(m_used[1], turn(SC2_1, KT - 1) + 1)
                        me(v.memset(B["qhi"][:].bitcast(F32), 0.0))
                        me(v.memset(B["qlo"][:].bitcast(F32), 0.0))
                        pair_queries(0)
                        me(v.memset(hb[:, 1, :], 0.0))
                        me.wait()
                        v.engine_nop().then_inc(sem("q_room"), 1)
            v.tensor_copy(h_hi[:, 1:PAIRS, :], B["k"][:, 1:PAIRS, :]).then_inc(sem("k_hi"), 1)
            dve.wait_ge(sem("nF"), 1)

            def decay_row(head):
                v.tensor_scalar(B["nFm"][:, head[1], :], B["nF"][:].bitcast(F32), two[:, ds(head[0], 1)], None, mult
                                ).then_inc(sem("nFm"), 1)

            def output(i, hh):
                dve.wait_ge(sem("ov"), 2 * i + hh + 1)
                r = slice(64 * hh, 64 * hh + 64)
                v.tensor_copy(B["q"][r, ds(i, 1), :].rearrange("p a n -> p (a n)"), ps[r, 6 + hh, :]
                              ).then_inc(sem("oc"), 1)

            def pair(i, first, last=False):
                def top(hh, tb):
                    dve.wait_ge(sem("S_mm"), 8 * i + 4 * hh + tb + 1)
                    v.tensor_reduce(st[:, 0, tb:tb + 1], ps[:, tb, 0:(tb + 1) * P], AX_X, mx, negate=True
                                    ).then_inc(sem("nmax"), 1)

                def scale(hh, tb):
                    dve.wait_ge(sem("Pe"), 8 * i + 4 * hh + tb + 1)
                    me(v.reciprocal(st[:, 2, tb:tb + 1], st[:, 1, tb:tb + 1]))
                    me.wait()
                    v.tensor_scalar(B["Pm"][:, tb, 0:(tb + 1) * P], B["Pm"][:, tb, 0:(tb + 1) * P],
                                    st[:, 2, tb:tb + 1], None, mult).then_inc(sem("Pn"), 1)

                for hh in range(2):
                    top(hh, 0)
                    decay_row((2 * i + hh + 1, 1 - hh))
                    if hh == 0 and not last:
                        pair_queries(i + 1)
                    top(hh, 1)
                    scale(hh, 0)
                    top(hh, 2)
                    scale(hh, 1)
                    top(hh, 3)
                    if hh == 1:
                        output(i, 0)
                    elif not first:
                        output(i - 1, 1)
                    scale(hh, 2)
                    scale(hh, 3)

            decay_row((0, 0))
            dve.wait_ge(sem("gp_mm2"), 1)
            fin_gate(4, G1_1 % ACC, 2).then_inc(sem("gp_ok"), 1)
            fin_cols(ps[:, 6, 0:16], SH2_1, SC2_1, "ffn1"
                     ).then_inc(sem("fin3"), 1)
            pair(0, True)
            with dve.Fori(1, PAIRS - 1) as i:
                me.loop(i, 8, 1)
                pair(i, False)
            me.end(PAIRS - 2)
            pair(PAIRS - 1, False, True)
            output(PAIRS - 1, 1)
            dve.wait_ge(sem("oc"), FH)
            for f in range(KT):
                me(v.tensor_copy(h_hi[:, f, :], B["q"][:, f, :]))
                me.wait()
                v.tensor_tensor(h_lo[:, f, :], B["q"][:, f, :], h_hi[:, f, :].bitcast(F32), sub
                                ).then_inc(sem("o"), 1)
            resid_norm(2, "3", G1_1 % ACC)
            ffn(1)
            resid_norm(3, None, G2_1 % ACC)

        @block.tensor
        def _(pe):
            t = nc.tensor

            def parts(order, s):
                pe.wait_ge(whi_ok[s], order + 1 + FREE)
                pe.wait_ge(wlo_ok[s], order + 1 + FREE)

            def three(dst, l_hi, l_lo, r_hi, r_lo, start, stop):
                t.matmul(dst, l_hi, r_lo, start=start, stop=False)
                t.matmul(dst, l_lo, r_hi, start=False, stop=False)
                return t.matmul(dst, l_hi, r_hi, start=False, stop=stop)

            def features(order, s, bank, arriving=None, gate_done=None):
                parts(order, s)
                whi = w_hi[:, s, :].rearrange("p (k n) -> p k n", k=KT)
                wlo = w_lo[:, s, :].rearrange("p (k n) -> p k n", k=KT)

                def product(m, k):
                    return three(ps[:, bank + m, :], whi[:, k, m * P:(m + 1) * P], wlo[:, k, m * P:(m + 1) * P],
                                 h_hi[:, k, :], h_lo[:, k, :], k == 0, k == KT - 1)

                if arriving is None:
                    for m in range(2):
                        for k in range(KT):
                            last = product(m, k)
                        if m == 0 and gate_done is not None:
                            last.then_inc(gate_done, 1)
                else:
                    for k in range(KT):
                        pe.wait_ge(sem(f"h{arriving}"), k + 1)
                        last = product(0, k)
                        if k == KT - 1 and gate_done is not None:
                            last.then_inc(gate_done, 1)
                        if k:
                            product(1, k - 1)
                    last = product(1, KT - 1)
                last.then_inc(w_used[s], 1)

            def tokens(order, bank):
                for s in range(2):
                    parts(order, s)
                    whi = w_hi[:, s, :].rearrange("p (k n) -> p k n", k=4)
                    wlo = w_lo[:, s, :].rearrange("p (k n) -> p k n", k=4)
                    for tt in range(TT):
                        for k4 in range(4):
                            k = 4 * s + k4
                            c = slice(tt * P, (tt + 1) * P)
                            last = three(ps[:, bank + tt, :], h_hi[:, k, c], h_lo[:, k, c], whi[:, k4, :],
                                         wlo[:, k4, :], k == 0, k == KT - 1)
                    last.then_inc(w_used[s], 1)

            def accumulated(u):
                pe.wait_ge(m_used[1], turn(u, KT - 1) + 1)

            def adaln_cols(bank, col, unit):
                for f in range(KT):
                    last = t.matmul(ps[:, bank, col + f:col + f + 1], acc[:, unit % ACC, f * P:(f + 1) * P],
                                    ones[:, 0:1], start=True, stop=True)
                return last

            def adaln_row(bank, unit):
                for half in range(2):
                    last = t.matmul(ps[:, bank + half, :], ones[:], acc[:, unit % ACC, half * HALF:(half + 1) * HALF],
                                    start=True, stop=True)
                return last

            def transpose(tag, src=None):
                for tt in range(TT):
                    pe.wait_ge(sem(f"xn{tag}"), tt + 1)
                    for k in range(KT):
                        tile = xt[tt % 2] if src is None else src[:, tt, :]
                        last = t.transpose(ps[:, k, tt * P:(tt + 1) * P], tile[:, k * P:(k + 1) * P], ident[:])
                        if tt == TT - 1 or k == KT - 1:
                            last.then_inc(sem(f"tr{tag}"), 1)

            def gate_mm(m, done):
                for k in range(KT):
                    last = three(ps[0:m, 4, :], gwh[:, k, 0:m], gwl[:, k, 0:m], h_hi[:, k, :], h_lo[:, k, :],
                                 k == 0, k == KT - 1)
                last.then_inc(done, 1)

            def out_proj(order, r, arriving):
                for g in range(2):
                    for s in range(2):
                        parts(order + g, s)
                        whi = w_hi[:, s, :].rearrange("p (k n) -> p k n", k=4)
                        wlo = w_lo[:, s, :].rearrange("p (k n) -> p k n", k=4)
                        turns = [(tt, k4) for tt in range(TT) for k4 in range(4)]
                        if g == 0 and s == 0:
                            turns[:8] = [(0, 0), (0, 1), (0, 2), (1, 0), (1, 1), (0, 3), (1, 2), (1, 3)]
                        for tt, k4 in turns:
                            k = 4 * s + k4
                            c = slice(tt * P, (tt + 1) * P)
                            if g == 0:
                                pe.wait_ge(arriving, max(k, 2 * tt + (tt > 0)) + 1)
                            last = three(ps[:, 2 * tt + g, :], h_hi[:, k, c], h_lo[:, k, c], whi[:, k4, :],
                                         wlo[:, k4, :], k == 0, k == KT - 1)
                            if g == 1 and s == 1 and k4 == 3:
                                last.then_inc(sem(f"y{r}"), 1)
                        if g == 0 or s == 0:
                            last.then_inc(w_used[s], 1)
                last_used(1, f"y{r}")

            def last_used(s, y):
                pe.wait_ge(sem(y), TT)
                pe.sem_inc(w_used[s], 1)

            def ffn(l):
                base = l * PERL // 2 + MIXBLK // 2
                down = (l * PERL + BIG) // 2
                r = 2 * l + 1
                def tile(i, s, arriving=None):
                    pe.wait_ge(sem(f"act{l}_{s}"), i + FREE)
                    features(base + i, s, 2 * s, arriving, sem(f"g{l}"))

                tile(0, 0, str(r))
                tile(0, 1)
                with pe.Fori(1, FT // 2 - 1) as i:
                    for s in range(2):
                        tile(i, s)
                tile(FT // 2 - 1, 0)
                accumulated((SC1_1, G2_1)[l])
                last = adaln_row(4, (G2_0, G2_1)[l])
                if l == 0:
                    for n, u in enumerate((KVSH, KVSC, SH1_1, SC1_1)):
                        last = adaln_cols(6, KT * n, u)
                last.then_inc(sem(f"gp_mm{r}"), 1)
                tile(FT // 2 - 1, 1)
                pe.wait_ge(sem("gp_ok"), 2 * l + 2)
                if l == 0:
                    pe.wait_ge(sem("fin2"), 1)

                def ktile(i, s, start):
                    parts(down + i, s)
                    pe.wait_ge(sem(f"alo{l}_{s}"), i + 1)
                    for tt in (0, 2, 3, 1) if start else range(TT):
                        if start and tt < 2:
                            pe.wait_ge(sem(f"act{l}_{tt}"), FT // 2 + FREE)
                        c = slice(tt * P, (tt + 1) * P)
                        for half in range(2):
                            n = slice(half * HALF, (half + 1) * HALF)
                            last = three(ps[:, 2 * tt + half, :], F["ahi"][:, s, c], F["alo"][:, s, c],
                                         w_hi[:, s, n], w_lo[:, s, n], start, False)
                    last.then_inc(w_used[s], 1)

                ktile(0, 0, True)
                ktile(0, 1, False)
                with pe.Fori(1, FT // 2 - 1) as i:
                    for s in range(2):
                        ktile(i, s, False)
                for tt, s in ((0, 0), (1, 0), (2, 0), (0, 1), (1, 1), (2, 1), (3, 0), (3, 1)):
                    if tt == 0:
                        parts(down + FT // 2 - 1, s)
                        pe.wait_ge(sem(f"alo{l}_{s}"), FT // 2)
                    c = slice(tt * P, (tt + 1) * P)
                    for half in range(2):
                        n = slice(half * HALF, (half + 1) * HALF)
                        last = three(ps[:, 2 * tt + half, :], F["ahi"][:, s, c], F["alo"][:, s, c],
                                     w_hi[:, s, n], w_lo[:, s, n], False, s == 1)
                    if s == 1:
                        last.then_inc(sem(f"y{r}"), 1)
                last_used(0, f"y{r}")
                last_used(1, f"y{r}")

            pe.wait_ge(setup_pool, 1)
            transpose("0")
            pe.wait_ge(acc_ok, 1)
            pe.wait_ge(sem("room"), 1)
            adaln_cols(KT - 1, 0, SH1_0)
            accumulated(SC1_0)
            adaln_cols(KT - 1, KT, SC1_0).then_inc(sem("fin_mm0"), 1)
            for i in range(2):
                for s in range(2):
                    n = 2 * i + s
                    if i:
                        pe.wait_ge(sem("qk"), n - 1)
                    features(i, s, 2 * s, "0" if i + s == 0 else None)
            pe.wait_ge(sem("gw_split"), 1)
            gate_mm(36, sem("gate_mm0"))
            pe.wait_ge(sem("qk"), 4)
            tokens(2, 0)
            pe.wait_ge(sem("lf"), 1)
            tokens(3, 4)
            pe.wait_ge(sem("v"), 4)
            tokens(4, 0)
            pe.wait_ge(sem("v"), 8)
            tokens(5, 4)
            pe.wait_ge(sem("og"), 4)
            pe.wait_ge(sem("em"), 1)
            for tt in range(TT):
                last = t.transpose(ps[:, 3, tt * 36:(tt + 1) * 36], G["G2"][0:36, tt * P:(tt + 1) * P],
                                   ident[0:36, 0:36])
            last.then_inc(sem("gt_mm"), 1)
            pe.wait_ge(sem("gc"), 1)

            def decay(h):
                pe.wait_ge(sem("Mh"), h + 1)
                if not (isinstance(h, int) and h == 0):
                    pe.wait_ge(sem("wT"), 4 * h)
                t.matmul(ps[:, 0, :], ones_r[:], A["Mh"][:], start=True, stop=True)
                t.matmul(ps[:, 3, :], ones_r[:], A["Mh"][:], start=True, stop=False)
                for tb in range(TT):
                    last = t.matmul(ps[:, 3, tb * P:(tb + 1) * P], identb[:], trib[:, 0, :], start=False,
                                    stop=tb == TT - 1)
                last.then_inc(sem("E"), 1)

            def key_query(h, tiles):
                pe.wait_ge(sem("kst"), h + 1)
                for sb_ in tiles:
                    q = A["qk"][:, ds(h, 1), :].rearrange("p a n -> p (a n)")[:, sb_ * P:S]
                    if not (isinstance(h, int) and h == 0 and sb_ < 2):
                        pe.wait_ge(sem(f"sT_{sb_ % 2}"), 2 * h + sb_ // 2)
                    t.matmul(ps[:, 1 + sb_ % 2, 0:S - sb_ * P], A["kst"][:, sb_ * P:(sb_ + 1) * P], q,
                             start=True, stop=True).then_inc(sem("kq"), 1)

            def numerator(h, ahead=None):
                if isinstance(h, int):
                    pe.wait_ge(sem("vlo"), MH)
                else:
                    pe.wait_ge(sem("vlo"), h + 1)
                for sb_ in range(TT):
                    pe.wait_ge(sem("sThi"), 4 * h + sb_ + 1)
                    pe.wait_ge(sem("sTlo"), 4 * h + sb_ + 1)
                    vhi = A["vhi"][:, sb_, ds(h, 1), :].rearrange("p a n -> p (a n)")
                    vlo = A["vlo"][:, sb_, ds(h, 1), :].rearrange("p a n -> p (a n)")[:, 0:DV]
                    for tt in range(sb_, TT):
                        c = slice(tt * P, (tt + 1) * P)
                        if sb_ == 0:
                            pe.wait_ge(sem("yh"), 4 * h + tt + 1)
                        t.matmul(ps[:, 4 + tt, 0:DVX], A["sTlo"][:, sb_, c], vhi, start=sb_ == 0, stop=False)
                        t.matmul(ps[:, 4 + tt, 0:DV], A["sT"][:, sb_, c], vlo, start=False, stop=False)
                        last = t.matmul(ps[:, 4 + tt, 0:DVX], A["sT"][:, sb_, c], vhi, start=False,
                                        stop=sb_ == tt)
                    last.then_inc(sem("sT_used"), 1)
                    if ahead is not None and sb_ in (1, 2):
                        key_query(ahead, [sb_ + 1])

            decay(0)
            key_query(0, range(2))
            pe.wait_ge(sem("og"), 8)
            accumulated(SC2_0)
            adaln_row(4, G1_0).then_inc(sem("row_mm0"), 1)
            key_query(0, range(2, TT))
            adaln_cols(6, 0, SH2_0)
            adaln_cols(6, KT, SC2_0).then_inc(sem("gp_mm0"), 1)
            with pe.Fori(0, MH - 1) as h:
                decay(h + 1)
                key_query(h + 1, range(2))
                pe.wait_ge(sem("gp_ok"), 1)
                pe.wait_ge(sem("fin1"), 1)
                numerator(h, h + 1)
            numerator(MH - 1)
            for h in range(MH):
                pe.wait_ge(sem("xny0"), TT * (h + 1))
                if h == 2:
                    pe.wait_ge(sem("yh"), (MH + 1) * TT)
                for tt in range(TT):
                    for k in (2 * h, 2 * h + 1):
                        last = t.transpose(ps[:, k, tt * P:(tt + 1) * P], A["og"][:, tt, k * P:(k + 1) * P], ident[:])
                last.then_inc(sem("try0"), 1)
            out_proj(6, 0, sem("hy0"))
            pe.wait_ge(sem("yread0"), TT)
            transpose("1", nx_all)
            ffn(0)
            pe.wait_ge(sem("yread1"), TT)
            transpose("2", nx_all)

            b0 = PERL // 2
            for i in range(2):
                for s in range(2):
                    if i:
                        pe.wait_ge(sem("k"), 2 * i + s - 1)
                    features(b0 + i, s, 2 * s, "2" if i + s == 0 else None)
            pe.wait_ge(sem("gw_split"), 2)
            gate_mm(FH, sem("gate_mm1"))
            pe.wait_ge(sem("k"), 4)
            tokens(b0 + 2, 0)
            pe.wait_ge(sem("nF"), 1)
            tokens(b0 + 3, 4)
            pe.wait_ge(sem("xnq"), TT)
            for group in range(2):
                if group == 1:
                    pe.wait_ge(sem("v1"), 8)
                for k in range(4 * group, 4 * group + 4):
                    for tt in range(TT):
                        last = t.transpose(ps[:, k, tt * P:(tt + 1) * P], nq[tt][:, k * P:(k + 1) * P], ident[:])
                    last.then_inc(sem("trq"), 1)
            for i in range(2):
                for s in range(2):
                    if i:
                        pe.wait_ge(sem("q"), 2 * i + s - 1)
                    features(b0 + 4 + i, s, 2 * s, "q" if i + s == 0 else None)
            accumulated(SC2_1)
            adaln_row(4, G1_1)
            adaln_cols(6, 0, SH2_1)
            adaln_cols(6, KT, SC2_1).then_inc(sem("gp_mm2"), 1)
            pe.wait_ge(sem("q"), 4)

            def scores(pair, hh, tb, first=False):
                n = (tb + 1) * P
                c = slice(tb * P, n)
                khi = h_hi[:, ds(pair, 1), :].rearrange("p a n -> p (a n)")[:, 0:n]
                klo = h_lo[:, ds(pair, 1), :].rearrange("p a n -> p (a n)")[:, 0:n]
                if tb == 0:
                    pe.wait_ge(sem("k_lo"), 1 if isinstance(pair, int) and pair == 0 else 2)
                    pe.wait_ge(sem("qlo"), 2 * pair + hh + 1)
                    pe.wait_ge(sem("nFm"), 2 * pair + hh + 1)
                if not first:
                    pe.wait_ge(sem("Pe"), 8 * pair + 4 * hh + tb - 3)
                t.matmul(ps[:, tb, 0:n], B["qhi"][:, hh, c], klo, start=True, stop=False)
                t.matmul(ps[:, tb, 0:n], B["qlo"][:, hh, c], khi, start=False, stop=False)
                t.matmul(ps[:, tb, 0:n], B["qhi"][:, hh, c], khi, start=False, stop=False)
                t.matmul(ps[:, tb, 0:n], ones_r[:], B["nFm"][:, hh, 0:n], start=False, stop=False)
                t.matmul(ps[:, tb, n - P:n], identb[:], trib[:, 1, :], start=False, stop=True
                         ).then_inc(sem("S_mm"), 1)

            def pair(i, first, last_pair):
                for hh in range(2):
                    for tb in range(TT):
                        m = 4 * hh + tb
                        pe.wait_ge(sem("Pn"), 8 * i + m + 1)
                        if not first or m >= 2:
                            pe.wait_ge(sem("PT"), 8 * i + m - 1)
                        for sb_ in range(tb + 1):
                            last = t.transpose(ps[:, 4 + tb % 2, sb_ * P:(sb_ + 1) * P],
                                               B["Pm"][:, tb, sb_ * P:(sb_ + 1) * P], ident[:])
                        last.then_inc(sem("PTps"), 1)
                        if hh == 0:
                            scores(i, 1, tb)
                        elif not last_pair:
                            scores(i + 1, 0, tb)
                    pe.wait_ge(sem("vst"), i + 1)
                    pe.wait_ge(sem("PT"), 8 * i + 4 * hh + 4)
                    if not first:
                        pe.wait_ge(sem("oc"), 2 * i + hh - 1)
                    for sb_ in range(TT):
                        last = t.matmul(ps[:, 6 + hh, sb_ * P:S], B["vst"][:, sb_, :], B["PT"][:, sb_, sb_ * P:S],
                                        start=sb_ == 0, stop=sb_ == TT - 1)
                    last.then_inc(sem("ov"), 1)

            for tb in range(TT):
                scores(0, 0, tb, first=True)
            pe.wait_ge(sem("fin3"), 1)
            pair(0, True, False)
            with pe.Fori(1, PAIRS - 1) as i:
                pair(i, False, False)
            pair(PAIRS - 1, False, True)
            out_proj(b0 + 6, 2, sem("o"))
            pe.wait_ge(sem("yread2"), TT)
            transpose("3", nx_all)
            ffn(1)


_SHAPE = (1, S, D)


def lay_out(a):
    f = np.float32

    def feat(w):
        n = w.shape[1] // (2 * P)
        return w.reshape(KT, P, n, 2 * P).transpose(2, 1, 0, 3).reshape(n, P, WBIG)

    def tok(w):
        n = w.shape[1] // HALF
        return w.reshape(2, 4, P, n, HALF).transpose(3, 0, 2, 1, 4).reshape(2 * n, P, WBIG)

    def up(w):
        return w.reshape(KT, P, 2, FT, P).transpose(3, 1, 0, 2, 4).reshape(FT, P, WBIG)

    aw, kw = a["a_w_in"][0], a["kv_w"]
    big = np.concatenate([
        feat(aw[:, :D]), tok(aw[:, D:3 * D]), tok(a["a_w_out"][0]), up(a["ffn_w_in"][0]),
        feat(kw[:, :D]), tok(kw[:, D:2 * D]), feat(a["b_w_q"][0]), tok(a["b_w_out"][0]), up(a["ffn_w_in"][1])])
    small = a["ffn_w_out"].reshape(2 * FT, P, D)
    order = [(0, 0), (0, 1), (0, 2), (0, 3), (0, 4), (0, 5), "k0", "k1", (1, 0), (1, 1), (1, 2), (1, 3), (1, 4), (1, 5)]
    mats, bias = [], []
    for o in order:
        m, b = (a["kv_mod_w"], a["kv_mod_b"]) if isinstance(o, str) else (a["mod_w"][o[0]], a["mod_b"][o[0]])
        j = int(o[1])
        mats.append(m[:, j * D:(j + 1) * D].reshape(KT, P, D))
        bias.append(b[j * D:(j + 1) * D])
    mods = np.concatenate(mats)
    gains = [a["mix_pre_g"][0], a["ffn_pre_g"][0], a["kv_norm_g"], a["mix_pre_g"][1], a["ffn_pre_g"][1],
             a["a_hnorm_g"][0], a["c"][0]]
    cols = np.zeros((P, NCOL), f)
    for i, vec in enumerate(bias + gains):
        cols[:, i * KT:(i + 1) * KT] = vec.reshape(KT, P).T
    cols[0:4, CMG] = a["a_gate_b"][0][:4]
    cols[32:36, CMG] = a["a_gate_b"][0][4:]
    cols[0:FH, CFG] = a["kv_fgate_b"]
    rows = np.stack([np.stack([bias[G1_0], a["mix_post_g"][0]]), np.stack([bias[G2_0], a["ffn_post_g"][0]]),
                     np.stack([bias[G1_1], a["mix_post_g"][1]]), np.stack([bias[G2_1], a["ffn_post_g"][1]])])
    gw0 = np.zeros((P, KT, 36), f)
    gate = aw[:, 3 * D:].reshape(KT, P, 2 * MH).transpose(1, 0, 2)
    gw0[:, :, 0:4], gw0[:, :, 32:36] = gate[:, :, :4], gate[:, :, 4:]
    gw1 = np.zeros((P, KT, 36), f)
    gw1[:, :, 0:FH] = kw[:, 2 * D:].reshape(KT, P, FH).transpose(1, 0, 2)
    return {"x_in": a["x"][0], "wbig": big, "wsmall": small, "mods": mods, "cols": cols, "rows": rows,
            "gw0": gw0, "gw1": gw1}


def kernel(**inputs):
    import concourse.bacc as bacc
    from concourse.bass_utils import run_bass_kernel_spmd

    arrays = {n: np.ascontiguousarray(v) for n, v in
              lay_out({n: np.asarray(v) for n, v in inputs.items()}).items()}
    nc = bacc.Bacc("TRN2", target_bir_lowering=False, num_devices=1)
    aps = [nc.dram_tensor(f"in_{n}", v.shape, F32, kind="ExternalInput").ap() for n, v in arrays.items()]
    out = nc.dram_tensor("out_y", (S, D), F32, kind="ExternalOutput").ap()
    build(nc, *aps, out)
    r = run_bass_kernel_spmd(nc, [{f"in_{n}": v for n, v in arrays.items()}], core_ids=[0])
    return r.results[0]["out_y"].reshape(_SHAPE)
```
